# Optimizing a Trainium2 kernel written in Bass

```python
import jax, jax.numpy as jnp
from jax import lax
import numpy as np

D_MODEL = 2048
BATCH = 1
SEQ = 512
DEPTH = 1

POOL_WIDTH = D_MODEL // 2
POOL_WINDOWS = (2, 4, 8, 16)
N_POOL_GROUPS = len(POOL_WINDOWS)
POOL_GROUP_DIM = POOL_WIDTH // N_POOL_GROUPS
MLSTM_WIDTH = D_MODEL
MLSTM_HEADS = 8
MLSTM_HEAD_DIM = MLSTM_WIDTH // MLSTM_HEADS
CHUNK = 128
N_EXPERTS = 16
EC_CAPACITY_FACTOR = 2
EXPERT_FF = D_MODEL // 2
N_GATE_COLS = 4 * MLSTM_HEADS
COL_POOL = 0
COL_Q = COL_POOL + POOL_WIDTH
COL_K = COL_Q + MLSTM_WIDTH
COL_V = COL_K + MLSTM_WIDTH
COL_O = COL_V + MLSTM_WIDTH
COL_IF = COL_O + MLSTM_WIDTH
COL_GP = COL_IF + N_GATE_COLS
COL_GM = COL_GP + D_MODEL
N_IN = COL_GM + D_MODEL
DEEPNORM_ALPHA = (2.0 * DEPTH) ** 0.25
DEEPNORM_BETA = (8.0 * DEPTH) ** -0.25
LN_EPS = 1e-5
GN_EPS = 1e-6

kernel_name = "pool_mlstm_ec_moe_deepnorm_encoder"

def layer_norm(x, g, b):
    xf = x.astype(jnp.float32)
    mu = jnp.mean(xf, axis=-1, keepdims=True)
    var = jnp.mean(jnp.square(xf - mu), axis=-1, keepdims=True)
    return ((xf - mu) * lax.rsqrt(var + LN_EPS) * g.astype(jnp.float32) + b.astype(jnp.float32)).astype(x.dtype)

def pool_mixer(u, w_grp, scale):
    bsz, seq, _ = u.shape
    t = jnp.arange(seq)
    ug = u.astype(jnp.float32).reshape(bsz, seq, N_POOL_GROUPS, POOL_GROUP_DIM)
    outs = []
    for grp, win in enumerate(POOL_WINDOWS):
        xg = ug[:, :, grp]
        cs = jnp.concatenate([jnp.zeros((bsz, 1, POOL_GROUP_DIM), jnp.float32),
                              jnp.cumsum(xg, axis=1)], axis=1)
        lo = jnp.clip(t - win // 2, 0, seq)
        hi = jnp.clip(t + win // 2, 0, seq)
        cnt = (hi - lo).astype(jnp.float32)[None, :, None]
        diff = (cs[:, hi] - cs[:, lo]) / cnt - xg
        outs.append(jnp.einsum('bsc,ce->bse', diff.astype(u.dtype), w_grp[grp]))
    return jnp.concatenate(outs, axis=-1) * scale

def mlstm_scan(q, k, v, log_i, log_f):
    bsz, nh, seq, dh = q.shape
    nc = seq // CHUNK

    def chunks(a):
        a = a.reshape((bsz, nh, nc, CHUNK) + a.shape[3:])
        return jnp.moveaxis(a, 2, 0)

    lower_tri = jnp.tril(jnp.ones((CHUNK, CHUNK), dtype=bool))

    def step(carry, xs):
        c_st, n_st, m_st = carry
        qc, kc, vc, ic, fc = xs
        b = jnp.cumsum(fc, axis=-1)
        g = b[..., -1]
        dmat = b[..., :, None] - b[..., None, :] + ic[..., None, :]
        dmat = jnp.where(lower_tri, dmat, -jnp.inf)
        inter = b + m_st[..., None]
        m_t = jnp.maximum(inter, jnp.max(dmat, axis=-1))
        a_mat = jnp.einsum('bhtk,bhsk->bhts', qc, kc) * jnp.exp(dmat - m_t[..., None])
        w_inter = jnp.exp(inter - m_t)
        num = (jnp.einsum('bhts,bhsv->bhtv', a_mat, vc)
               + w_inter[..., None] * jnp.einsum('bhvk,bhtk->bhtv', c_st, qc))
        den = jnp.sum(a_mat, axis=-1) + w_inter * jnp.einsum('bhk,bhtk->bht', n_st, qc)
        h = num / jnp.maximum(jnp.abs(den), jnp.exp(-m_t))[..., None]
        a_log = g[..., None] - b + ic
        m_new = jnp.maximum(g + m_st, jnp.max(a_log, axis=-1))
        decay = jnp.exp(g + m_st - m_new)
        wa = jnp.exp(a_log - m_new[..., None])
        c_new = decay[..., None, None] * c_st + jnp.einsum('bhsv,bhsk->bhvk', vc * wa[..., None], kc)
        n_new = decay[..., None] * n_st + jnp.einsum('bhs,bhsk->bhk', wa, kc)
        return (c_new, n_new, m_new), h

    carry0 = (jnp.zeros((bsz, nh, dh, dh), jnp.float32),
              jnp.zeros((bsz, nh, dh), jnp.float32),
              jnp.zeros((bsz, nh), jnp.float32))
    _, hs = lax.scan(step, carry0, (chunks(q), chunks(k), chunks(v), chunks(log_i), chunks(log_f)))
    return jnp.moveaxis(hs, 0, 2).reshape(bsz, nh, seq, dh)

def mlstm_mixer(q, k, v, o, gate_pre, b_if, norm_w):
    bsz, seq, _ = q.shape

    def heads(a):
        return a.astype(jnp.float32).reshape(bsz, seq, MLSTM_HEADS, MLSTM_HEAD_DIM).transpose(0, 2, 1, 3)

    qh = heads(q) * (MLSTM_HEAD_DIM ** -0.5)
    kh = heads(k)
    vh = heads(v)
    gts = (gate_pre.astype(jnp.float32) + b_if.astype(jnp.float32)).transpose(0, 2, 1)
    i_f, f_f, i_b, f_b = jnp.split(gts, 4, axis=1)
    h_fwd = mlstm_scan(qh, kh, vh, i_f, jax.nn.log_sigmoid(f_f))
    flip = lambda a: jnp.flip(a, axis=2)
    h_bwd = flip(mlstm_scan(flip(qh), flip(kh), flip(vh), flip(i_b), flip(jax.nn.log_sigmoid(f_b))))
    h = h_fwd + h_bwd
    mu = jnp.mean(h, axis=-1, keepdims=True)
    var = jnp.mean(jnp.square(h - mu), axis=-1, keepdims=True)
    hn = ((h - mu) * lax.rsqrt(var + GN_EPS)).transpose(0, 2, 1, 3).reshape(bsz, seq, MLSTM_WIDTH)
    hn = hn * norm_w.astype(jnp.float32)
    return (jax.nn.sigmoid(o.astype(jnp.float32)) * hn).astype(q.dtype)

def expert_choice_moe(x, w_router, w_gate, w_up, w_down):
    bsz, seq, dm = x.shape
    cap = EC_CAPACITY_FACTOR * seq // N_EXPERTS
    aff = jax.nn.softmax((x @ w_router).astype(jnp.float32), axis=-1)
    gate, idx = lax.top_k(aff.transpose(0, 2, 1), cap)
    xe = jax.vmap(lambda xb, ib: xb[ib])(x, idx)
    hid = (jax.nn.silu(jnp.einsum('becd,edf->becf', xe, w_gate))
           * jnp.einsum('becd,edf->becf', xe, w_up))
    y = jnp.einsum('becf,efd->becd', hid, w_down) * gate[..., None].astype(x.dtype)
    return jax.vmap(lambda ib, yb: jnp.zeros((seq, dm), y.dtype)
                    .at[ib.reshape(-1)].add(yb.reshape(-1, dm)))(idx, y)

def setup_inputs(seed: int = 0) -> dict:
    key = jax.random.key(seed)
    ks = jax.random.split(key, 20)
    f32 = jnp.float32
    nrm = lambda k, shape, s: jax.random.normal(k, shape, f32) * s
    x = jax.random.normal(ks[0], (BATCH, SEQ, D_MODEL), f32)
    w_in = nrm(ks[1], (DEPTH, D_MODEL, N_IN), D_MODEL ** -0.5)
    i_bias = nrm(ks[2], (DEPTH, MLSTM_HEADS), 0.1)
    f_bias = jnp.linspace(3.0, 6.0, MLSTM_HEADS, dtype=f32)[None, :] + nrm(ks[3], (DEPTH, MLSTM_HEADS), 0.1)
    i_bias_b = nrm(ks[4], (DEPTH, MLSTM_HEADS), 0.1)
    f_bias_b = jnp.linspace(3.0, 6.0, MLSTM_HEADS, dtype=f32)[None, :] + nrm(ks[5], (DEPTH, MLSTM_HEADS), 0.1)
    b_if = jnp.concatenate([i_bias, f_bias, i_bias_b, f_bias_b], axis=-1)
    w_pool_grp = nrm(ks[6], (DEPTH, N_POOL_GROUPS, POOL_GROUP_DIM, POOL_GROUP_DIM), POOL_GROUP_DIM ** -0.5)
    pool_scale = 1.0 + nrm(ks[7], (DEPTH, POOL_WIDTH), 0.1)
    w_pool_up = nrm(ks[8], (DEPTH, POOL_WIDTH, D_MODEL), POOL_WIDTH ** -0.5)
    mlstm_norm_w = 1.0 + nrm(ks[9], (DEPTH, MLSTM_WIDTH), 0.02)
    w_mlstm_up = nrm(ks[10], (DEPTH, MLSTM_WIDTH, D_MODEL), MLSTM_WIDTH ** -0.5)
    w_out = nrm(ks[11], (DEPTH, D_MODEL, D_MODEL), D_MODEL ** -0.5 * DEEPNORM_BETA)
    ln1_g = 1.0 + nrm(ks[12], (DEPTH, D_MODEL), 0.02)
    ln1_b = nrm(ks[13], (DEPTH, D_MODEL), 0.02)
    w_router = nrm(ks[14], (DEPTH, D_MODEL, N_EXPERTS), D_MODEL ** -0.5)
    w_gate = nrm(ks[15], (DEPTH, N_EXPERTS, D_MODEL, EXPERT_FF), D_MODEL ** -0.5)
    w_up = nrm(ks[16], (DEPTH, N_EXPERTS, D_MODEL, EXPERT_FF), D_MODEL ** -0.5)
    w_down = nrm(ks[17], (DEPTH, N_EXPERTS, EXPERT_FF, D_MODEL), EXPERT_FF ** -0.5 * DEEPNORM_BETA)
    ln2_g = 1.0 + nrm(ks[18], (DEPTH, D_MODEL), 0.02)
    ln2_b = nrm(ks[19], (DEPTH, D_MODEL), 0.02)
    return {"x": x, "w_in": w_in, "b_if": b_if, "w_pool_grp": w_pool_grp, "pool_scale": pool_scale,
            "w_pool_up": w_pool_up, "mlstm_norm_w": mlstm_norm_w, "w_mlstm_up": w_mlstm_up,
            "w_out": w_out, "ln1_g": ln1_g, "ln1_b": ln1_b, "w_router": w_router,
            "w_gate": w_gate, "w_up": w_up, "w_down": w_down, "ln2_g": ln2_g, "ln2_b": ln2_b}

def reference(x, w_in, b_if, w_pool_grp, pool_scale, w_pool_up, mlstm_norm_w, w_mlstm_up,
              w_out, ln1_g, ln1_b, w_router, w_gate, w_up, w_down, ln2_g, ln2_b):
    for layer in range(DEPTH):
        wl = w_in[layer]
        proj = lambda lo, hi: x @ wl[:, lo:hi]
        pool_in = proj(COL_POOL, COL_Q)
        q = proj(COL_Q, COL_K)
        k = proj(COL_K, COL_V)
        v = proj(COL_V, COL_O)
        o = proj(COL_O, COL_IF)
        gate_pre = proj(COL_IF, COL_GP)
        gp = jax.nn.sigmoid(proj(COL_GP, COL_GM))
        gm = jax.nn.sigmoid(proj(COL_GM, N_IN))
        y_pool = pool_mixer(pool_in, w_pool_grp[layer], pool_scale[layer]) @ w_pool_up[layer]
        y_mlstm = mlstm_mixer(q, k, v, o, gate_pre, b_if[layer], mlstm_norm_w[layer]) @ w_mlstm_up[layer]
        mix = (gp * y_pool + gm * y_mlstm) @ w_out[layer]
        x = layer_norm(DEEPNORM_ALPHA * x + mix, ln1_g[layer], ln1_b[layer])
        ffn = expert_choice_moe(x, w_router[layer], w_gate[layer], w_up[layer], w_down[layer])
        x = layer_norm(DEEPNORM_ALPHA * x + ffn, ln2_g[layer], ln2_b[layer])
    return x


_drawn_inputs = setup_inputs


def setup_inputs(seed=0):
    import zlib

    import numpy as np

    out = dict(_drawn_inputs(seed))
    spreads = {}
    factors = {'mlstm_norm_w': 8.0, 'ln1_g': 2.69, 'ln1_b': 2.706, 'ln2_g': 2.84, 'ln2_b': 2.912}
    for name, (base, spread) in spreads.items():
        noise = np.random.default_rng([zlib.crc32(name.encode()), seed]).standard_normal(out[name].shape)
        drawn = base * np.exp(spread * noise) if base else spread * noise
        out[name] = __import__('jax').numpy.asarray(drawn.astype(out[name].dtype))
    for name, factor in factors.items():
        out[name] = (out[name] * factor).astype(out[name].dtype)
    return out
```

```python
from contextlib import ExitStack

import concourse.bass as bass
from concourse import mybir
from concourse.alu_op_type import AluOpType as ALU

F32 = mybir.dt.float32
F32R = mybir.dt.float32r
U32 = mybir.dt.uint32
ACT = mybir.ActivationFunctionType
AX = mybir.AxisListType

P = 128
S = 512
D = 2048
TT = S // P
KT = D // P
CW = 512
SK = 4
NCH = D // CW
PW = D // 2
WINDOWS = (2, 4, 8, 16)
GD = PW // len(WINDOWS)
PAD = max(WINDOWS) // 2
HEADS = 8
HD = D // HEADS
PAIRS = HEADS // 2
NE = 16
CAP = 2 * S // NE
FF = D // 2
FT = FF // P
EP = NE // 2
COL_Q = PW
COL_K = COL_Q + D
COL_V = COL_K + D
COL_O = COL_V + D
COL_IF = COL_O + D
NG = 4 * HEADS
COL_GP = COL_IF + NG
COL_GM = COL_GP + D
ALPHA = 2.0 ** 0.25
LN_EPS = 1e-5
GN_EPS = 1e-6
NEG = -1e30

RAW = 4
HL = 2
RAW_M = 6
HL_M = 3
AHEAD_M = HL_M - 1

G_POOL = 0
G_A = G_POOL + 2 * 4
G_B = G_A + NCH * (4 + 2)
G_C = G_B + PAIRS * 5 * 4
G_D = G_C + NCH * 4
G_END = G_D + NCH * 4
U_POOL = 0
U_A = 2
U_B = U_A + 2 * NCH
U_C = U_B + 5 * PAIRS
U_D = U_C + NCH

F_OFF = [0, 512, 896, 1152]
B_OFF = [0, 128, 384, 768]
TRI = 1280


def f_range(i):
    return P * i, S - P * i


def b_range(i):
    return 0, P * (i + 1)


class Order:

    def __init__(self, eng, sem):
        self.eng, self.sem, self.n, self.turn = eng, sem, 0, 0

    def add(self, ins):
        ins.then_inc(self.sem, 1)
        self.n += 1

    def wait(self):
        self.eng.wait_ge(self.sem, self.turn + self.n)

    def loop(self, i, per):
        self.start, self.per, self.turn = self.n, per, i * per

    def end(self, trips):
        assert self.n - self.start == self.per, (self.n - self.start, self.per)
        self.n, self.turn = self.start + self.per * trips, 0


def build(nc, io):
    (x, w_in, b_if, w_pool_grp, pool_scale, w_pool_up, mlstm_norm_w, w_mlstm_up, w_out, ln1_g, ln1_b,
     w_router, w_gate, w_up, w_down, ln2_g, ln2_b, out) = io

    def dram(name, shape):
        return nc.dram_tensor(name, shape, F32, kind="Internal").ap()

    gate_rows_d = dram("gate_rows_d", (2, HEADS, S))
    zp_d = dram("zp_d", (D, S))
    sgm_d = dram("sgm_d", (D, S))
    hg_d = dram("hg_d", (D, S))
    x1_d = dram("x1_d", (S, D))

    def tiles_of_rows(w):
        return w.rearrange("(k p) n -> p k n", p=P)

    w_in_v, pool_up_v = tiles_of_rows(w_in[0]), tiles_of_rows(w_pool_up[0])
    mlstm_up_v, w_out_v = tiles_of_rows(w_mlstm_up[0]), tiles_of_rows(w_out[0])
    zp_v, sgm_v, hg_v = tiles_of_rows(zp_d), tiles_of_rows(sgm_d), tiles_of_rows(hg_d)
    x_v, out_v = tiles_of_rows(x[0]), tiles_of_rows(out[0])
    gate_v = w_gate[0].rearrange("e (k p) n -> p e k n", p=P)
    up_v = w_up[0].rearrange("e (k p) n -> p e k n", p=P)
    down_v = w_down[0].rearrange("e (k p) n -> p e k n", p=P)

    keep = ExitStack()
    keep.__enter__()

    def on(stack, name, shape, dt=F32):
        return stack.enter_context(nc.sbuf_tensor(name, [P, *shape], dt))

    def sb(name, shape, dt=F32):
        return on(keep, name, shape, dt)

    raw = [sb(f"raw{n}", [SK * CW]) for n in range(RAW)]
    whi = [sb(f"whi{n}", [SK, CW], F32R) for n in range(HL)]
    wlo = [sb(f"wlo{n}", [SK, CW], F32R) for n in range(HL)]
    ident = sb("ident", [P])
    halves = sb("halves", [CAP])
    slot_no = sb("slot_no", [P])
    behind = sb("behind", [2, P])
    token_no = sb("token_no", [TT])
    bias_if = sb("bias_if", [NG])
    a_col = sb("a_col", [HEADS, 2, TT])
    em_col = sb("em_col", [HEADS, 2, TT])
    nw_col = sb("nw_col", [KT])
    ps_col = sb("ps_col", [PW // P])
    den = sb("den", [2, TT])
    stat = sb("stat", [TT, NCH, 6])
    mv = sb("mv", [TT, 2])
    rstd = sb("rstd", [TT])
    nmr = sb("nmr", [TT])
    geps = sb("geps", [1])
    leps = sb("leps", [1])
    carrier = sb("carrier", [1])
    credit = sb("credit", [8])
    part = ExitStack()
    xhi = on(part, "xhi", [KT, S], F32R)
    xlo = on(part, "xlo", [KT, S], F32R)
    sub = ExitStack()
    xst = on(sub, "xst", [NCH, TT, CW])
    wif = on(sub, "wif", [KT, NG])
    wif_hi = on(sub, "wif_hi", [KT, NG], F32R)
    wif_lo = on(sub, "wif_lo", [KT, NG], F32R)
    sub.close()
    g_ones = on(sub, "g_ones", [S])
    g_f = on(sub, "g_f", [2, S])
    g_a = on(sub, "g_a", [2, S])
    g_m = on(sub, "g_m", [2, S])
    g_em = on(sub, "g_em", [2, S])
    g_neg = on(sub, "g_neg", [2, S])
    gate_pre = on(sub, "gate_pre", [TT, NG])
    gate_tmp = on(sub, "gate_tmp", [3, TT, 2, HEADS])
    sub.close()
    pmhi = on(sub, "pmhi", [PW // P, S], F32R)
    pmlo_a = on(sub, "pmlo_a", [PW // P // 2, S], F32R)
    late = ExitStack()
    grp_raw = on(late, "grp_raw", [2, 4 * GD])
    late.close()
    pmlo_b = on(sub, "pmlo_b", [PW // P // 2, S], F32R)
    late = ExitStack()
    dhi = on(late, "dhi", [4, S], F32R)
    dlo = on(late, "dlo", [4, S], F32R)
    pool_u = on(late, "pool_u", [4, S + 2 * PAD])
    sum_a = on(late, "sum_a", [2, S + 2 * PAD])
    sum_b = on(late, "sum_b", [2, S + 2 * PAD])
    redge = on(late, "redge", [len(WINDOWS), 2 * PAD])
    grp_hi = on(late, "grp_hi", [4 * GD], F32R)
    grp_lo = on(late, "grp_lo", [4 * GD], F32R)
    late.close()
    sgp = on(late, "sgp", [4, S])
    zt = on(late, "zt", [4, S])
    late.close()
    sub.close()
    kT = on(sub, "kT", [4, S])
    qT = on(sub, "qT", [4, S])
    vv = on(sub, "vv", [TT, 2, HD + 1])
    so = on(sub, "so", [4, S])
    amat = [on(sub, f"amat{h}", [2, TRI]) for h in range(2)]
    gb = on(sub, "gb", [2, S])
    gd = on(sub, "gd", [2, S])
    hh = [on(sub, f"hh{h}", [TT, HD]) for h in range(2)]
    sgm = on(sub, "sgm", [4, S])
    sub.close()
    part.close()
    hghi = on(part, "hghi", [KT, S], F32R)
    hglo = on(part, "hglo", [KT, S], F32R)
    hraw = on(sub, "hraw", [NCH, 4, S])
    sub.close()
    zhi = on(sub, "zhi", [KT, S], F32R)
    zlo = on(sub, "zlo", [KT, S], F32R)
    late = ExitStack()
    cz = on(late, "cz", [2, 2, S])
    late.close()
    xc = on(late, "xc", [TT, CW])
    late.close()
    sub.close()
    part.close()
    acc = on(part, "acc", [TT, D])
    raw_new = [on(part, f"raw{n}", [SK * CW]) for n in range(RAW, RAW_M)]
    lng1 = on(sub, "lng1", [D])
    lnb1 = on(sub, "lnb1", [D])
    sub.close()
    raw_m = raw_new + raw
    whi_m = [on(part, "whi2", [SK, CW], F32R)] + whi
    wlo_m = [on(part, "wlo2", [SK, CW], F32R)] + wlo
    slot_c = on(part, "slot_c", [TT, NE])
    aff_c = on(part, "aff_c", [TT, NE])
    x1T = [on(sub, f"x1T{n}", [KT, P]) for n in range(2)]
    wr = on(sub, "wr", [KT, NE])
    sm_max = on(sub, "sm_max", [1])
    sm_sum = on(sub, "sm_sum", [1])
    sm_rec = on(sub, "sm_rec", [1])
    sm_exp = on(sub, "sm_exp", [NE])
    aff_r = on(sub, "aff_r", [S])
    work = [on(sub, f"work{n}", [S]) for n in range(2)]
    top8 = on(sub, "top8", [8])
    picked = on(sub, "picked", [S])
    slot_r = on(sub, "slot_r", [S])
    r_ones = on(sub, "r_ones", [S])
    sub.close()
    xe = on(part, "xe", [D])
    xeT = on(part, "xeT", [KT, 2, P], F32R)
    gu = on(part, "gu", [2, FF])
    onehot = on(part, "onehot", [2, TT, P])
    scat = on(part, "scat", [2, S], F32R)
    gate_w = on(part, "gate_w", [2])
    tok_f = on(part, "tok_f", [1])
    tok_u = on(part, "tok_u", [1], U32)
    hid_tmp = on(part, "hid_tmp", [CW])
    hid = [on(part, f"hid{e}", [FT, P], F32R) for e in range(2)]
    yhi = on(part, "yhi", [2, CW], F32R)
    ylo = on(part, "ylo", [2, CW], F32R)
    lng2 = on(part, "lng2", [D])
    lnb2 = on(part, "lnb2", [D])
    part.close()

    def pmlo(k):
        half = PW // P // 2
        return (pmlo_a if k < half else pmlo_b)[:, k % half, :]

    ps = keep.enter_context(nc.psum_tensor("ps", [P, 8, CW], F32))
    U = [ps[:, n, :] for n in range(4)]
    X = [ps[:, 4 + n, :] for n in range(4)]
    Xall = ps[:, 4:8, :]

    def sem(name):
        return keep.enter_context(nc.semaphore(name))

    raw_in = [sem(f"raw_in{n}") for n in range(RAW)]
    raw_in_m = [sem(f"raw_in_m{n}") for n in range(RAW_M)]
    hi_done = sem("hi_done")
    lo_done = sem("lo_done")
    sub_done = sem("sub_done")
    unit_out = sem("unit_out")
    consts = sem("consts")
    x_in = [sem(f"x_in{n}") for n in range(NCH)]
    par_in = sem("par_in")
    xT_ps, xT_hi, xT_lo = sem("xT_ps"), sem("xT_hi"), sem("xT_lo")
    wif_h, wif_l = sem("wif_h"), sem("wif_l")
    gate_ps, pre_rdy, soft_rdy, gate_rdy = sem("gate_ps"), sem("pre_rdy"), sem("soft_rdy"), sem("gate_rdy")
    rows_ps, neg_rdy, m_rdy, em_rdy = sem("rows_ps"), sem("neg_rdy"), sem("m_rdy"), sem("em_rdy")
    neg_st, col_ps, col_rdy = sem("neg_st"), sem("col_ps"), sem("col_rdy")
    grp_in, grph, grpl, grp_ps = sem("grp_in"), sem("grph"), sem("grpl"), sem("grp_ps")
    diff_rdy, dhi_rdy, dlo_rdy = sem("diff_rdy"), sem("dhi_rdy"), sem("dlo_rdy")
    pm_hi, pm_lo = sem("pm_hi"), sem("pm_lo")
    zp_st = sem("zp_st")
    zt_free, so_free, sgm_free = sem("zt_free"), sem("so_free"), sem("sgm_free")
    v_ones = sem("v_ones")
    gb_in, gd_rdy, e_rdy, s_ps, a_rdy = sem("gb_in"), sem("gd_rdy"), sem("e_rdy"), sem("s_ps"), sem("a_rdy")
    av_ps, den_abs, rec_rdy, hf_rdy = sem("av_ps"), sem("den_abs"), sem("rec_rdy"), sem("hf_rdy")
    var_rdy, sq_rdy, hn_rdy = sem("var_rdy"), sem("sq_rdy"), sem("hn_rdy")
    ht_ps, hg_rdy, hg_st, sgm_st = sem("ht_ps"), sem("hg_rdy"), sem("hg_st"), sem("sgm_st")
    hraw_in = [sem(f"hraw_in{n}") for n in range(NCH)]
    hgs_hi, hgs_lo = sem("hgs_hi"), sem("hgs_lo")
    cz_in = [sem(f"cz_in{n}") for n in range(2)]
    z_rdy, z_hi, z_lo = sem("z_rdy"), sem("z_hi"), sem("z_lo")
    xc_in = sem("xc_in")
    dve, act, pool = sem("dve"), sem("act"), sem("pool")
    var1_rdy, sq1_rdy, rst_rdy = sem("var1_rdy"), sem("sq1_rdy"), sem("rst_rdy")
    ln_in, ln2_in, ln_nrm, x1_rdy, x1_st = sem("ln_in"), sem("ln2_in"), sem("ln_nrm"), sem("x1_rdy"), sem("x1_st")
    wr_in, x1T_ps, x1T_rdy = sem("wr_in"), sem("x1T_ps"), sem("x1T_rdy")
    lg_ps, lg_max, lg_exp, aff_rdy = sem("lg_ps"), sem("lg_max"), sem("lg_exp"), sem("aff_rdy")
    affT_ps, slot_rdy, slotT_ps, acc_scaled = sem("affT_ps"), sem("slot_rdy"), sem("slotT_ps"), sem("acc_scaled")
    oh_rdy, tok_ps, tok_cp, tok_rdy = sem("oh_rdy"), sem("tok_ps"), sem("tok_cp"), sem("tok_rdy")
    xe_in, xeT_ps, xeT_hi, xeT_lo = sem("xe_in"), sem("xeT_ps"), sem("xeT_hi"), sem("xeT_lo")
    scat_ps, scat_rdy, gw_ps, gw_rdy = sem("scat_ps"), sem("scat_rdy"), sem("gw_ps"), sem("gw_rdy")
    slots_free = sem("slots_free")
    gu_rdy, guT_ps, sig_rdy, silu_rdy, hid_pre = (sem("gu_rdy"), sem("guT_ps"), sem("sig_rdy"), sem("silu_rdy"),
                                                  sem("hid_pre"))
    hid_hi, hid_lo, y_hi, y_lo = sem("hid_hi"), sem("hid_lo"), sem("y_hi"), sem("y_lo")
    comb_ps, acc_add = sem("comb_ps"), sem("acc_add")
    o_var, o_sq, o_rst, o_nrm, o_rdy, out_st = (sem("o_var"), sem("o_sq"), sem("o_rst"), sem("o_nrm"),
                                               sem("o_rdy"), sem("out_st"))

    ahead = [zt_free, so_free, sgm_free, hg_rdy, hid_lo, y_lo, comb_ps, acc_add]

    class Spare:

        def __init__(self, eng):
            self.eng, self.reg = eng, eng.alloc_register("count")
            eng.reg_mov(self.reg, 0)

        def take_wait(self):
            self.eng.reg_add(self.reg, self.reg, 1)
            self.eng.reg_add(self.reg, self.reg, 1)

        def end(self):
            self.eng.wait_ge(lo_done, self.eng.snap(self.reg))

    block = keep.enter_context(nc.Block())

    @block.sync
    def _(sp):
        def load_stage(base, i, per, k, src):
            if base + k >= RAW:
                sp.wait_ge(lo_done, i * per + (base + k - RAW + 1))
            sp.dma_start(raw[k % RAW][:, :].rearrange("p (k n) -> p k n", k=SK), src).then_inc(raw_in[k % RAW], 16)

        for c in range(NCH):
            sp.dma_start(xst[:, c, :, :], x_v[:, :, c * CW:(c + 1) * CW]).then_inc(x_in[c], 16)
        for k in range(8):
            u, s = k // 4, k % 4
            load_stage(G_POOL, 0, 0, k, w_in_v[:, SK * s:SK * s + SK, u * CW:(u + 1) * CW])
        with sp.Fori(1, NCH // 2 + 1) as after:
            i = after - 1
            for j in range(2):
                for s in range(4):
                    load_stage(G_A, i, 12, 6 * j + s,
                               w_in_v[:, SK * s:SK * s + SK, bass.ds(i * (2 * CW) + (COL_GP + j * CW), CW)])
                for s in range(2):
                    load_stage(G_A, i, 12, 6 * j + 4 + s,
                               pool_up_v[:, SK * s:SK * s + SK, bass.ds(after * (2 * CW) + (j - 2) * CW, CW)])
        with sp.Fori(0, PAIRS) as i:
            for n, col in enumerate((COL_K, COL_Q, COL_V, COL_O, COL_GM)):
                for s in range(4):
                    load_stage(G_B, i, 20, 4 * n + s, w_in_v[:, SK * s:SK * s + SK, bass.ds(i * CW + col, CW)])
        for base, w in ((G_C, mlstm_up_v), (G_D, w_out_v)):
            with sp.Fori(0, NCH) as i:
                for s in range(4):
                    load_stage(base, i, 4, s, w[:, SK * s:SK * s + SK, bass.ds(i * CW, CW)])

        def expert_load(i, k, src):
            sp.wait_ge(lo_done, i * 48 + (G_END + k - RAW_M + 1))
            sp.dma_start(raw_m[k % RAW_M][:, :].rearrange("p (k n) -> p k n", k=SK),
                         src.rearrange("p e k n -> p (e k) n")).then_inc(raw_in_m[k % RAW_M], 16)

        sp.wait_ge(sub_done, 4 * G_D)
        with sp.Fori(0, EP) as i:
            for e in range(2):
                for n, w in enumerate((gate_v, up_v)):
                    for c in range(2):
                        for s in range(4):
                            expert_load(i, 16 * e + 8 * n + 4 * c + s,
                                        w[:, bass.ds(2 * i + e, 1), SK * s:SK * s + SK, c * CW:(c + 1) * CW])
            for c in range(NCH):
                for e in range(2):
                    for s in range(2):
                        expert_load(i, 32 + 4 * c + 2 * e + s,
                                    down_v[:, bass.ds(2 * i + e, 1), SK * s:SK * s + SK, c * CW:(c + 1) * CW])
        for t in range(TT):
            sp.wait_ge(o_rdy, t + 1)
            sp.dma_start(out_v[:, t, :], acc[:, t, :]).then_inc(out_st, 16)
        sp.wait_ge(out_st, 16 * TT)

    @block.gpsimd
    def _(pl):
        order = Order(pl, pool)
        spare = Spare(pl)
        pl.dma_start(wif[:, :, :], w_in_v[:, :, COL_IF:COL_IF + NG]).then_inc(par_in, 16)
        pl.dma_start(bias_if[:, :], b_if[0:1, :].to_broadcast((P, NG))).then_inc(par_in, 16)
        pl.dma_start(ps_col[:, :], pool_scale[0].rearrange("(k p) -> p k", p=P),
                     allow_slow_non_contiguous=True).then_inc(par_in, 16)
        pl.dma_start(nw_col[:, :], mlstm_norm_w[0].rearrange("(k p) -> p k", p=P),
                     allow_slow_non_contiguous=True).then_inc(par_in, 16)
        order.add(pl.memset(ident[:, :], 0.0))
        order.add(pl.memset(halves[:, :], 0.0))
        order.add(pl.memset(behind[:, :, :], 0.0))
        order.wait()
        for d, sign in ((0, 1), (1, -1)):
            order.add(pl.affine_select(out=behind[:, d, :], in_=behind[:, d, :], compare_op=ALU.is_ge, fill=NEG,
                                       base=0, pattern=[[sign, P]], channel_multiplier=-sign))
        order.add(pl.affine_select(out=ident[:, :], in_=ident[:, :], compare_op=ALU.not_equal, fill=1.0, base=0,
                                   pattern=[[-1, P]], channel_multiplier=1))
        order.add(pl.affine_select(out=halves[:, :], in_=halves[:, :], compare_op=ALU.not_equal, fill=1.0, base=0,
                                   pattern=[[-1, CAP]], channel_multiplier=1))
        order.wait()
        pl.affine_select(out=halves[:, :], in_=halves[:, :], compare_op=ALU.not_equal, fill=1.0,
                         base=-CAP, pattern=[[-1, CAP]], channel_multiplier=1).then_inc(consts, 1)
        pl.iota(slot_no[:, :], pattern=[[0, 2], [1, CAP]], base=0, channel_multiplier=0,
                allow_small_or_imprecise_dtypes=True).then_inc(consts, 1)
        pl.iota(token_no[:, :], pattern=[[P, TT]], base=0, channel_multiplier=1,
                allow_small_or_imprecise_dtypes=True).then_inc(consts, 1)
        order.add(pl.memset(redge[:, :, :], 0.0))
        order.wait()
        for w, win in enumerate(WINDOWS):
            h = win // 2
            for t in range(PAD):
                order.add(pl.memset(redge[:, w, t:t + 1], 1.0 / (min(t, h) + h)))
            for t in range(S - PAD, S):
                c = PAD + t - (S - PAD)
                order.add(pl.memset(redge[:, w, c:c + 1], 1.0 / (min(S - t, h) + h)))
        order.wait()
        pl.memset(pool_u[:, :, 0:PAD], 0.0).then_inc(consts, 1)
        pl.memset(pool_u[:, :, PAD + S:], 0.0).then_inc(consts, 1)
        for n, s_ in enumerate(ahead):
            pl.memset(credit[:, n:n + 1], 0.0).then_inc(s_, 1)
        pl.wait_ge(xT_ps, KT)
        pl.dma_start(grp_raw[:, :, :], w_pool_grp[0].rearrange("(j g) (c p) n -> p j (g c) n", j=2, p=P))\
          .then_inc(grp_in, 16)
        pl.wait_ge(neg_rdy, 1)
        pl.dma_start(gate_rows_d.rearrange("d h s -> h d s"), g_neg[0:HEADS, :, :]).then_inc(neg_st, 16)

        def stored(st, i, free):
            col = ahead.index(free)
            pl.wait_ge(st, 16 * i + 16)
            pl.wait_ge(free, i + 1)
            pl.tensor_tensor(credit[:, col:col + 1], ident[:, 0:1], ident[:, 0:1], ALU.add).then_inc(free, 1)

        with pl.Fori(0, NCH) as i:
            pl.wait_ge(unit_out, 8 * i + (4 * U_A + 8))
            pl.dma_start(zp_v[:, bass.ds(4 * i, 4), :], zt[:, :, :]).then_inc(zp_st, 16)
            stored(zp_st, i, zt_free)
        pl.wait_ge(sub_done, 4 * G_B)
        pl.wait_ge(neg_st, 16)
        pl.wait_ge(zp_st, 16 * NCH)
        pl.memset(vv[:, :, :, HD:HD + 1], 1.0).then_inc(v_ones, 1)
        with pl.Fori(0, PAIRS) as i:
            for h in range(2):
                if h:
                    pl.wait_ge(e_rdy, 28 * i + 14)
                src = gate_rows_d[:, bass.ds(2 * i + h, 1), :].rearrange("d h s -> h d s")
                pl.dma_start(gb[:, :, :], src.to_broadcast((P, 2, S))).then_inc(gb_in, 16)
                pl.wait_ge(gb_in, 32 * i + 16 * (h + 1))
                for d in range(2):
                    pl.tensor_tensor(gd[:, d, :].rearrange("p (t n) -> p t n", t=TT),
                                     gb[:, d, :].rearrange("p (t n) -> p t n", t=TT),
                                     behind[:, d:d + 1, :].to_broadcast((P, TT, P)), ALU.add).then_inc(gd_rdy, 1)
            pl.wait_ge(hg_rdy, 4 * i + 4 + 1)
            pl.dma_start(hg_v[:, bass.ds(4 * i, 4), :], so[:, :, :]).then_inc(hg_st, 16)
            pl.wait_ge(unit_out, 20 * i + (4 * U_B + 20))
            spare.take_wait()
            pl.dma_start(sgm_v[:, bass.ds(4 * i, 4), :], sgm[:, :, :]).then_inc(sgm_st, 16)
            stored(hg_st, i, so_free)
            stored(sgm_st, i, sgm_free)
        pl.wait_ge(hg_st, 16 * PAIRS)
        for c in range(NCH):
            pl.dma_start(hraw[:, c, :, :], hg_v[:, 4 * c:4 * c + 4, :]).then_inc(hraw_in[c], 16)
        pl.wait_ge(sgm_st, 16 * PAIRS)

        def load_cz(i, s):
            pl.dma_start(cz[:, s % 2, 0:1, :], sgm_v[:, bass.ds(4 * i + s, 1), :]).then_inc(cz_in[s % 2], 16)
            pl.dma_start(cz[:, s % 2, 1:2, :], zp_v[:, bass.ds(4 * i + s, 1), :]).then_inc(cz_in[s % 2], 16)

        load_cz(0, 0)
        load_cz(0, 1)
        with pl.Fori(0, NCH - 1) as i:
            for s in range(4):
                pl.wait_ge(z_lo, 4 * i + s + 1)
                load_cz(i, s + 2)
        for s in range(2):
            pl.wait_ge(z_lo, 4 * (NCH - 1) + s + 1)
            load_cz(NCH - 1, s + 2)
        pl.wait_ge(z_lo, KT)
        with pl.Fori(0, NCH) as i:
            pl.wait_ge(unit_out, 4 * i + 4 * U_D)
            pl.dma_start(xc[:, :, :], x_v[:, :, bass.ds(i * CW, CW)]).then_inc(xc_in, 16)
        pl.dma_start(lng1[:, :], ln1_g[0:1, :].to_broadcast((P, D))).then_inc(ln_in, 16)
        pl.dma_start(lnb1[:, :], ln1_b[0:1, :].to_broadcast((P, D))).then_inc(ln_in, 16)
        pl.wait_ge(sub_done, 4 * G_END)
        pl.dma_start(wr[:, :, :], tiles_of_rows(w_router[0])).then_inc(wr_in, 16)
        pl.wait_ge(unit_out, 4 * (U_D + NCH))
        pl.dma_start(lng2[:, :], ln2_g[0:1, :].to_broadcast((P, D))).then_inc(ln2_in, 16)
        pl.dma_start(lnb2[:, :], ln2_b[0:1, :].to_broadcast((P, D))).then_inc(ln2_in, 16)
        for t in range(TT):
            pl.wait_ge(x1_rdy, t + 1)
            pl.dma_start(x1_d[t * P:(t + 1) * P, :], acc[:, t, :]).then_inc(x1_st, 16)
        pl.wait_ge(x1_st, 16 * TT)

        def gather():
            pl.indirect_dma_start(xe[:, :], None, x1_d, bass.IndirectOffsetOnAxis(ap=tok_u[:, 0:1], axis=0))\
              .then_inc(xe_in, 16)

        pl.wait_ge(tok_rdy, 1)
        gather()
        with pl.Fori(1, EP) as i:
            pl.wait_ge(xeT_ps, 4 * i)
            pl.wait_ge(tok_rdy, i + 1)
            spare.take_wait()
            gather()
        spare.end()

    @block.tensor
    def _(pe):
        mm = nc.tensor.matmul

        def transpose(o, src, n=P):
            return nc.tensor.transpose(o, src, ident[0:n, 0:n])

        pe.wait_ge(consts, 5)
        for kt in range(KT):
            if kt % SK == 0:
                pe.wait_ge(x_in[kt // SK], 16)
            if kt >= 8:
                pe.wait_ge(xT_lo, kt - 7)
            for t in range(TT):
                c = kt % SK
                last = transpose(ps[:, kt % 8, t * P:(t + 1) * P], xst[:, kt // SK, t, c * P:(c + 1) * P])
            last.then_inc(xT_ps, 1)
        pe.wait_ge(xT_lo, KT)
        pe.wait_ge(wif_l, 1)
        for t in range(TT):
            o, tok = X[0][:, t * NG:(t + 1) * NG], slice(t * P, (t + 1) * P)
            for kt in range(KT):
                mm(o, xhi[:, kt, tok], wif_hi[:, kt, :], start=kt == 0, stop=False)
                mm(o, xhi[:, kt, tok], wif_lo[:, kt, :], start=False, stop=False)
                last = mm(o, xlo[:, kt, tok], wif_hi[:, kt, :], start=False, stop=kt == KT - 1)
        last.then_inc(gate_ps, 1)

        def stage(base, i, per, k, s, n_stages, natural, mhi, mlo, unit):
            pe.wait_ge(lo_done, i * per + (base + k + 1))
            for sub_ in range(4):
                if s == 0 and (per or unit):
                    pe.wait_ge(unit_out, unit * 4 - 3 + sub_)
                cols = slice(sub_ * P, (sub_ + 1) * P)
                for r in range(SK):
                    kt = SK * s + r
                    first, stop = kt == 0, kt == SK * n_stages - 1
                    wh, wl = whi[k % HL][:, r, :], wlo[k % HL][:, r, :]
                    ah, al = mhi(kt), mlo(kt)
                    if natural:
                        mm(U[sub_], ah[:, cols], wh, start=first, stop=False)
                        mm(U[sub_], ah[:, cols], wl, start=False, stop=False)
                        last_ = mm(U[sub_], al[:, cols], wh, start=False, stop=stop)
                    else:
                        mm(U[sub_], wh[:, cols], ah, start=first, stop=False)
                        mm(U[sub_], wh[:, cols], al, start=False, stop=False)
                        last_ = mm(U[sub_], wl[:, cols], ah, start=False, stop=stop)
                last_.then_inc(sub_done, 1)

        def row_tile(a):
            return lambda kt: a[:, kt, :]

        X_IN = (row_tile(xhi), row_tile(xlo))
        PM_IN = (row_tile(pmhi), pmlo)

        def pool_groups(j):
            pe.wait_ge(dlo_rdy, 2 * j + 2)
            pe.wait_ge(grpl, j + 1)
            for gg in range(2):
                for es in range(2):
                    n = 2 * gg + es
                    for ct in range(2):
                        w = slice((gg * 2 + ct) * GD + es * P, (gg * 2 + ct) * GD + (es + 1) * P)
                        a = 2 * gg + ct
                        mm(X[n], grp_hi[:, w], dhi[:, a, :], start=ct == 0, stop=False)
                        mm(X[n], grp_hi[:, w], dlo[:, a, :], start=False, stop=False)
                        last_ = mm(X[n], grp_lo[:, w], dhi[:, a, :], start=False, stop=ct == 1)
                    last_.then_inc(grp_ps, 1)

        for s in range(4):
            stage(G_POOL, 0, 0, s, s, 4, False, *X_IN, 0)
        pe.wait_ge(gate_rdy, 1)
        for k in range(4):
            for t in range(TT):
                last = transpose(X[k][0:HEADS, t * P:(t + 1) * P], gate_pre[:, t, HEADS * k:HEADS * (k + 1)])
        last.then_inc(rows_ps, 1)
        for s in range(4):
            if s == 2:
                pe.wait_ge(em_rdy, 1)
                for kind, src in ((0, g_a), (1, g_em)):
                    for d in range(2):
                        for t in range(TT):
                            n = ((kind * 2 + d) * TT + t) * HEADS
                            last = transpose(X[0][:, n:n + HEADS], src[0:HEADS, d, t * P:(t + 1) * P], HEADS)
                last.then_inc(col_ps, 1)
            if s == 3:
                pe.wait_ge(col_rdy, 2)
                pool_groups(0)
            stage(G_POOL, 0, 0, 4 + s, s, 4, False, *X_IN, 1)
        pe.wait_ge(pm_lo, 4)
        pool_groups(1)
        pe.wait_ge(pm_lo, 8)
        with pe.Fori(0, NCH // 2) as i:
            for j in range(2):
                for s in range(4):
                    stage(G_A, i, 12, 6 * j + s, s, 4, False, *X_IN, 4 * i + (U_A + 2 * j))
                for s in range(2):
                    stage(G_A, i, 12, 6 * j + 4 + s, s, 2, False, *PM_IN, 4 * i + (U_A + 2 * j + 1))

        def scores(h):
            for kt in range(TT):
                for c in range(2):
                    last_ = mm(X[kt], kT[:, 2 * h + c, kt * P:(kt + 1) * P], qT[:, 2 * h + c, :],
                               start=c == 0, stop=c == 1)
                last_.then_inc(s_ps, 1)

        def values(h, d):
            for qt in range(TT):
                keys = range(qt + 1) if d == 0 else range(qt, TT)
                for kt in keys:
                    at = (F_OFF[kt] + (qt - kt) * P) if d == 0 else (B_OFF[kt] + qt * P)
                    last_ = mm(X[qt][:, 0:HD + 1], amat[h][:, d, at:at + P], vv[:, kt, h, :],
                               start=kt == keys[0], stop=kt == keys[-1])
                last_.then_inc(av_ps, 1)

        def head_back(h):
            for c in range(2):
                for t in range(TT):
                    last_ = transpose(X[c][:, t * P:(t + 1) * P], hh[h][:, t, c * P:(c + 1) * P])
                last_.then_inc(ht_ps, 1)

        with pe.Fori(0, PAIRS) as i:
            for k in range(20):
                if k == 9:
                    pe.wait_ge(unit_out, 20 * i + 4 * (U_B + 2))
                    pe.wait_ge(hg_rdy, 4 * i + 1)
                    scores(0)
                if k == 11:
                    pe.wait_ge(a_rdy, 16 * i + 8)
                    scores(1)
                if k == 13:
                    pe.wait_ge(a_rdy, 16 * i + 16)
                    pe.wait_ge(unit_out, 20 * i + 4 * (U_B + 3))
                    pe.wait_ge(v_ones, 1)
                    values(0, 0)
                if k == 14:
                    pe.wait_ge(hf_rdy, 8 * i + 4)
                    values(0, 1)
                if k == 15:
                    pe.wait_ge(hn_rdy, 8 * i + 4)
                    values(1, 0)
                if k == 16:
                    pe.wait_ge(hf_rdy, 8 * i + 8)
                    values(1, 1)
                if k == 17:
                    pe.wait_ge(hn_rdy, 8 * i + 8)
                    head_back(0)
                if k == 18:
                    pe.wait_ge(hg_rdy, 4 * i + 2 + 1)
                    head_back(1)
                stage(G_B, i, 20, k, k % 4, 4, k // 4 == 2, *X_IN, 5 * i + (U_B + k // 4))
        with pe.Fori(0, NCH) as i:
            for s in range(4):
                pe.wait_ge(hgs_lo, s + 1)
                stage(G_C, i, 4, s, s, 4, False, row_tile(hghi), row_tile(hglo), i + U_C)
        pe.wait_ge(z_lo, KT)
        with pe.Fori(0, NCH) as i:
            for s in range(4):
                stage(G_D, i, 4, s, s, 4, True, row_tile(zhi), row_tile(zlo), i + U_D)

        pe.wait_ge(unit_out, 4 * (U_D + NCH))
        pe.wait_ge(wr_in, 16)
        for t in range(TT):
            pe.wait_ge(x1_rdy, t + 1)
            if t >= 2:
                pe.wait_ge(aff_rdy, t - 1)
            for b in range(4):
                for r in range(4):
                    kt = 4 * b + r
                    last = transpose(ps[:, 4 * (t % 2) + b, r * P:(r + 1) * P], acc[:, t, kt * P:(kt + 1) * P])
                last.then_inc(x1T_ps, 1)
            pe.wait_ge(x1T_rdy, 4 * t + 4)
            for kt in range(KT):
                last = mm(ps[:, 4 * (t % 2), 0:NE], x1T[t % 2][:, kt, :], wr[:, kt, :], start=kt == 0,
                          stop=kt == KT - 1)
            last.then_inc(lg_ps, 1)
        pe.wait_ge(aff_rdy, TT)
        for t in range(TT):
            last = transpose(X[1][0:NE, t * P:(t + 1) * P], aff_c[:, t, :])
        last.then_inc(affT_ps, 1)
        pe.wait_ge(slot_rdy, 1)
        for t in range(TT):
            last = transpose(X[0][:, t * NE:(t + 1) * NE], slot_r[0:NE, t * P:(t + 1) * P], NE)
            if t < TT - 1:
                last.then_inc(slots_free, 1)
        last.then_inc(slotT_ps, 1)

        def tokens_of_slots(q):
            pe.wait_ge(oh_rdy, 8 * q + 8)
            for e in range(2):
                for t in range(TT):
                    last_ = mm(X[2][e * CAP:(e + 1) * CAP, 0:1], onehot[:, e, t, 0:CAP], token_no[:, t:t + 1],
                               start=t == 0, stop=t == TT - 1)
            last_.then_inc(tok_ps, 1)

        def gathered_back(q):
            pe.wait_ge(xe_in, 16 * q + 16)
            for b in range(4):
                for r in range(4):
                    kt = 4 * b + r
                    last_ = transpose(X[b][:, r * P:(r + 1) * P], xe[:, kt * P:(kt + 1) * P])
                last_.then_inc(xeT_ps, 1)

        tokens_of_slots(0)
        pe.wait_ge(tok_rdy, 1)
        gathered_back(0)
        pe.wait_ge(xeT_lo, 4)

        def scatter_and_weights(q):
            for e in range(2):
                for t in range(TT):
                    last_ = transpose(X[e][:, t * P:(t + 1) * P], onehot[:, e, t, :])
                last_.then_inc(scat_ps, 1)
            for e in range(2):
                for t in range(TT):
                    last_ = mm(X[3][:, e:e + 1], onehot[:, e, t, :], aff_c[:, t, bass.ds(2 * q + e, 1)],
                               start=t == 0, stop=t == TT - 1)
            last_.then_inc(gw_ps, 1)

        def halves_added():
            for n in range(2):
                for f in range(FT):
                    last_ = mm(X[n][:, f * CAP:(f + 1) * CAP], gu[:, n, f * P:(f + 1) * P], halves[:, :],
                               start=True, stop=True)
                last_.then_inc(guT_ps, 1)

        def combine():
            for t in range(TT):
                for e in range(2):
                    w = scat[:, e, t * P:(t + 1) * P]
                    mm(X[t], w, yhi[:, e, :], start=e == 0, stop=False)
                    last_ = mm(X[t], w, ylo[:, e, :], start=False, stop=e == 1)
                last_.then_inc(comb_ps, 1)

        def expert_pair(q, last_pair):
            for k in range(48):
                if k == 1:
                    pe.wait_ge(acc_add, 4 * q + 1)
                    scatter_and_weights(q)
                if k == 17:
                    pe.wait_ge(scat_rdy, 2 * q + 2)
                    pe.wait_ge(gu_rdy, 8 * q + 4)
                    halves_added()
                if k == 20 and not last_pair:
                    tokens_of_slots(q + 1)
                if k == 33:
                    pe.wait_ge(hid_pre, 2 * q + 1)
                    pe.wait_ge(gu_rdy, 8 * q + 8)
                    halves_added()
                if k in (37, 41, 45):
                    c = (k - 37) // 4
                    pe.wait_ge(y_lo, 8 * q + 2 * c + 2 + 1)
                    if c == 0:
                        pe.wait_ge(hid_pre, 2 * q + 2)
                        pe.wait_ge(gw_rdy, q + 1)
                        if not last_pair:
                            pe.wait_ge(tok_rdy, q + 2)
                    else:
                        pe.wait_ge(acc_add, 4 * q + c + 1)
                    combine()
                if k == 46 and not last_pair:
                    pe.wait_ge(acc_add, 4 * q + 3 + 1)
                    gathered_back(q + 1)
                pe.wait_ge(lo_done, 48 * q + (G_END + k + 1))
                wh, wl = whi_m[k % HL_M], wlo_m[k % HL_M]
                if k < 32:
                    e, c, s, depth = k // 16, k % 16 // 4, k % 4, KT
                    bank = U[c]
                    if k == 0:
                        pe.wait_ge(xeT_lo, 4 * q + 4)
                        pe.wait_ge(y_lo, 8 * q + 1)
                    if k >= 16 and s == 0:
                        pe.wait_ge(gu_rdy, 8 * q + 1 + c)
                    acts = [xeT[:, SK * s + r, e, :] for r in range(SK)]
                else:
                    c, e, s, depth = (k - 32) // 4, (k - 32) % 4 // 2, k % 2, FT
                    bank = U[2 * e + c % 2]
                    if s == 0 and c == 0:
                        pe.wait_ge(hid_lo, 2 * q + e + 1 + 1)
                        pe.wait_ge(gu_rdy, 8 * q + 5)
                    if s == 0 and c >= 2:
                        pe.wait_ge(y_lo, 8 * q + 2 * (c - 2) + e + 1 + 1)
                    acts = [hid[e][:, SK * s + r, :] for r in range(SK)]
                for r in range(SK):
                    n = SK * s + r
                    mm(bank, acts[r], wh[:, r, :], start=n == 0, stop=False)
                    last_ = mm(bank, acts[r], wl[:, r, :], start=False, stop=n == depth - 1)
                last_.then_inc(slots_free, 1)
            pe.wait_ge(y_lo, 8 * q + 8 + 1)
            pe.wait_ge(acc_add, 4 * q + 3 + 1)
            if not last_pair:
                pe.wait_ge(xeT_lo, 4 * q + 8)
            combine()

        with pe.Fori(0, EP - 1) as i:
            expert_pair(i, False)
        expert_pair(EP - 1, True)

    @block.scalar
    def _(sc):
        A = nc.scalar.activation
        order = Order(sc, act)

        def split(base, i, per, k):
            n = base + k
            sc.wait_ge(raw_in[k % RAW], i * (16 * (per // RAW)) + 16 * (n // RAW + 1))
            if n >= HL:
                sc.wait_ge(sub_done, i * (4 * per) + 4 * (n - HL + 1))
            A(whi[k % HL][:, :, :].rearrange("p k n -> p (k n)"), raw[k % RAW][:, :], ACT.Copy).then_inc(hi_done, 1)

        def read_out(base, i, per, k, dst, func):
            for sub_ in range(4):
                sc.wait_ge(sub_done, i * (4 * per) + (4 * (base + k) + sub_ + 1))
                A(dst(sub_), U[sub_], func).then_inc(unit_out, 1)

        sc.wait_ge(par_in, 64)
        A(wif_hi[:, :, :], wif[:, :, :], ACT.Copy).then_inc(wif_h, 1)
        for kt in range(KT):
            sc.wait_ge(xT_ps, kt + 1)
            A(xhi[:, kt, :], ps[:, kt % 8, :], ACT.Copy).then_inc(xT_hi, 1)
        split(G_POOL, 0, 0, 0)
        f_gates = gate_pre[:, :, :].rearrange("p t (d k h) -> p t d k h", d=2, k=2)[:, :, :, 1, :]
        sc.wait_ge(pre_rdy, TT)
        order.add(A(gate_tmp[:, 0], f_gates, ACT.Abs))
        order.wait()
        order.add(A(gate_tmp[:, 1], gate_tmp[:, 0], ACT.Exp, scale=-1.0))
        order.wait()
        A(gate_tmp[:, 2], gate_tmp[:, 1], ACT.Ln, bias=1.0).then_inc(soft_rdy, 1)

        def group_weights(j):
            sc.wait_ge(grp_in, 16)
            if j:
                sc.wait_ge(grp_ps, 4)
            A(grp_hi[:, :], grp_raw[:, j, :], ACT.Copy).then_inc(grph, 1)

        def differences(j):
            for gg in range(2):
                sc.wait_ge(diff_rdy, 2 * j + gg + 1)
                if j:
                    sc.wait_ge(grp_ps, 4)
                src = (sum_a if gg == 0 else sum_b)[:, :, PAD:PAD + S]
                A(dhi[:, 2 * gg:2 * gg + 2, :], src, ACT.Copy).then_inc(dhi_rdy, 1)

        def groups_out(j):
            for n in range(4):
                sc.wait_ge(grp_ps, 4 * j + n + 1)
                A(pmhi[:, 4 * j + n, :], X[n], ACT.Copy, scale=ps_col[:, 4 * j + n:4 * j + n + 1]).then_inc(pm_hi, 1)

        for k in range(8):
            split(G_POOL, 0, 0, k + 1)
            if k == 3:
                read_out(G_POOL, 0, 0, k, lambda n: pool_u[:, n, PAD:PAD + S], ACT.Copy)
            if k == 4:
                sc.wait_ge(m_rdy, 1)
                A(g_em[0:HEADS, :, :], g_m[0:HEADS, :, :], ACT.Exp, scale=-1.0).then_inc(em_rdy, 1)
                group_weights(0)
            if k == 5:
                differences(0)
            if k == 7:
                sc.wait_ge(neg_st, 16)
                groups_out(0)
                group_weights(1)
                sc.wait_ge(dlo_rdy, 2)
                read_out(G_POOL, 0, 0, k, lambda n: pool_u[:, n, PAD:PAD + S], ACT.Copy)
        differences(1)
        groups_out(1)
        with sc.Fori(0, NCH // 2) as i:
            for k in range(12):
                split(G_A, i, 12, k + 1)
                if k % 6 == 3:
                    read_out(G_A, i, 12, k, lambda n: sgp[:, n, :], ACT.Sigmoid)

        def decays(i, h):
            sc.wait_ge(gd_rdy, 4 * i + 2 * h + 2)
            for kt in range(TT):
                for d in range(2):
                    bias = a_col[:, bass.ds(2 * i + h, 1), d, kt:kt + 1].rearrange("p a b -> p (a b)")
                    own = slice(kt * P, (kt + 1) * P)
                    off = F_OFF[kt] if d == 0 else B_OFF[kt]
                    here = off if d == 0 else off + kt * P
                    A(amat[h][:, d, here:here + P], gd[:, d, own], ACT.Exp, bias=bias).then_inc(e_rdy, 1)
                    rest = slice((kt + 1) * P, S) if d == 0 else slice(0, kt * P)
                    n = rest.stop - rest.start
                    if n:
                        there = off + P if d == 0 else off
                        A(amat[h][:, d, there:there + n], gb[:, d, rest], ACT.Exp, bias=bias).then_inc(e_rdy, 1)

        def denominator(i, h, d):
            sc.wait_ge(av_ps, 16 * i + 8 * h + 4 * d + 4)
            A(den[:, d, :], Xall[:, :, HD], ACT.Abs).then_inc(den_abs, 1)

        def forward_out(i, h):
            sc.wait_ge(rec_rdy, 4 * i + 2 * h + 1)
            for t in range(TT):
                A(hh[h][:, t, :], X[t][:, 0:HD], ACT.Copy, scale=den[:, 0, t:t + 1]).then_inc(hf_rdy, 1)

        def head_root(i, h):
            sc.wait_ge(var_rdy, 2 * i + h + 1)
            A(rstd[:, :], mv[:, :, 1], ACT.Sqrt, bias=geps[:, 0:1]).then_inc(sq_rdy, 1)

        with sc.Fori(0, PAIRS) as i:
            for k in range(20):
                split(G_B, i, 20, k + 1)
                if k == 3:
                    sc.wait_ge(v_ones, 1)
                    read_out(G_B, i, 20, k, lambda n: kT[:, n, :], ACT.Copy)
                if k == 7:
                    read_out(G_B, i, 20, k, lambda n: qT[:, n, :], ACT.Copy)
                if k == 8:
                    decays(i, 0)
                if k == 10:
                    decays(i, 1)
                if k == 11:
                    read_out(G_B, i, 20, k, lambda n: vv[:, n, :, 0:HD], ACT.Copy)
                if k == 13:
                    denominator(i, 0, 0)
                    forward_out(i, 0)
                if k == 14:
                    denominator(i, 0, 1)
                    head_root(i, 0)
                if k == 15:
                    denominator(i, 1, 0)
                    forward_out(i, 1)
                    sc.wait_ge(so_free, i + 1)
                    read_out(G_B, i, 20, k, lambda n: so[:, n, :], ACT.Sigmoid)
                if k == 16:
                    denominator(i, 1, 1)
                    head_root(i, 1)
                if k == 19:
                    sc.wait_ge(sgm_free, i + 1)
                    read_out(G_B, i, 20, k, lambda n: sgm[:, n, :], ACT.Sigmoid)
        for c in range(NCH):
            sc.wait_ge(hraw_in[c], 16)
            A(hghi[:, 4 * c:4 * c + 4, :], hraw[:, c, :, :], ACT.Copy).then_inc(hgs_hi, 1)

        def z_parts(i):
            for n in range(4):
                sc.wait_ge(z_rdy, 4 * i + n + 1)
                A(zhi[:, bass.ds(4 * i + n, 1), :], cz[:, n % 2, 1:2, :], ACT.Copy).then_inc(z_hi, 1)

        with sc.Fori(0, NCH) as i:
            for k in range(4):
                split(G_C, i, 4, k + 1)
                if k == 3:
                    z_parts(i)
        with sc.Fori(0, NCH - 1) as i:
            for k in range(4):
                split(G_D, i, 4, k + 1)
        for k in range(3):
            split(G_D + 4 * (NCH - 1), 0, 0, k + 1)

        sc.wait_ge(var1_rdy, 1)
        A(rstd[:, :], mv[:, :, 1], ACT.Sqrt, bias=leps[:, 0:1]).then_inc(sq1_rdy, 1)
        sc.wait_ge(rst_rdy, 1)
        for t in range(TT):
            A(acc[:, t, :], acc[:, t, :], ACT.Identity, bias=nmr[:, t:t + 1], scale=rstd[:, t:t + 1])\
                .then_inc(ln_nrm, 1)
        for t in range(TT):
            for b in range(4):
                sc.wait_ge(x1T_ps, 4 * t + b + 1)
                A(x1T[t % 2][:, 4 * b:4 * b + 4, :], ps[:, 4 * (t % 2) + b, :], ACT.Copy).then_inc(x1T_rdy, 1)
            sc.wait_ge(lg_max, t + 1)
            A(sm_exp[:, :], ps[:, 4 * (t % 2), 0:NE], ACT.Exp, bias=sm_max[:, 0:1], accum_out=sm_sum[:, 0:1])\
                .then_inc(lg_exp, 1)
        sc.wait_ge(x1_st, 16 * TT)
        for t in range(TT):
            A(acc[:, t, :], acc[:, t, :], ACT.Copy, scale=ALPHA).then_inc(acc_scaled, 1)

        def split_m(q, k):
            sc.wait_ge(raw_in_m[k % RAW_M], q * (16 * 48 // RAW_M) + 16 * (k // RAW_M + 1))
            sc.wait_ge(slots_free, 48 * q + (k + 1))
            A(whi_m[k % HL_M][:, :, :].rearrange("p k n -> p (k n)"), raw_m[k % RAW_M][:, :], ACT.Copy)\
                .then_inc(hi_done, 1)

        def tokens_hi(q):
            for b in range(4):
                sc.wait_ge(xeT_ps, 4 * q + b + 1)
                A(xeT[:, 4 * b:4 * b + 4, :, 0:CAP], X[b].rearrange("p (r e n) -> p r e n", r=4, e=2), ACT.Copy)\
                    .then_inc(xeT_hi, 1)

        def hidden(q, e):
            sc.wait_ge(guT_ps, 4 * q + 2 * e + 1)
            sc.wait_ge(hid_lo, 2 * q + e + 1)
            A(hid_tmp[:, :], X[0], ACT.Sigmoid).then_inc(sig_rdy, 1)
            sc.wait_ge(hid_pre, 2 * q + e + 1)
            A(hid[e][:, :, 0:CAP], hid_tmp[:, :].rearrange("p (f n) -> p f n", f=FT), ACT.Copy).then_inc(hid_hi, 1)

        def expert_pair(q, last_pair):
            for k in range(AHEAD_M):
                split_m(q, k)
            for k in range(48):
                if k + AHEAD_M < 48:
                    split_m(q, k + AHEAD_M)
                if k == 1:
                    for e in range(2):
                        sc.wait_ge(scat_ps, 2 * q + e + 1)
                        A(scat[:, e, :], X[e], ACT.Copy).then_inc(scat_rdy, 1)
                if k < 32 and k % 4 == 3:
                    c = k % 16 // 4
                    sc.wait_ge(slots_free, 48 * q + (k + 1 + HL_M))
                    A(gu[:, c // 2, c % 2 * CW:(c % 2 + 1) * CW], U[c], ACT.Copy).then_inc(gu_rdy, 1)
                if k == 17:
                    hidden(q, 0)
                if k == 33:
                    hidden(q, 1)
                if k >= 32 and k % 2 == 1:
                    c, e = (k - 32) // 4, (k - 32) % 4 // 2
                    sc.wait_ge(slots_free, 48 * q + (k + 1 + HL_M))
                    sc.wait_ge(gw_rdy, q + 1)
                    sc.wait_ge(comb_ps, 16 * q + 4 * c + 1)
                    A(yhi[:, e, :], U[2 * e + c % 2], ACT.Copy, scale=gate_w[:, e:e + 1]).then_inc(y_hi, 1)
                if k == 46 and not last_pair:
                    tokens_hi(q + 1)

        tokens_hi(0)
        with sc.Fori(0, EP - 1) as i:
            expert_pair(i, False)
        expert_pair(EP - 1, True)
        sc.wait_ge(o_var, 1)
        A(rstd[:, :], mv[:, :, 1], ACT.Sqrt, bias=leps[:, 0:1]).then_inc(o_sq, 1)
        sc.wait_ge(o_rst, 1)
        for t in range(TT):
            A(acc[:, t, :], acc[:, t, :], ACT.Identity, bias=nmr[:, t:t + 1], scale=rstd[:, t:t + 1])\
                .then_inc(o_nrm, 1)

    @block.vector
    def _(ve):
        V = nc.vector
        order = Order(ve, dve)

        def less(o, a, hi):
            return V.tensor_tensor(o, a, hi.bitcast(F32), ALU.subtract)

        def split(base, i, per, k):
            ve.wait_ge(hi_done, i * per + (base + k + 1))
            less(wlo[k % HL][:, :, :].rearrange("p k n -> p (k n)"), raw[k % RAW][:, :],
                 whi[k % HL][:, :, :].rearrange("p k n -> p (k n)")).then_inc(lo_done, 1)

        order.add(V.memset(geps[:, :], GN_EPS))
        order.add(V.memset(leps[:, :], LN_EPS))
        ve.wait_ge(wif_h, 1)
        less(wif_lo[:, :, :], wif[:, :, :], wif_hi[:, :, :]).then_inc(wif_l, 1)
        for kt in range(KT):
            ve.wait_ge(xT_hi, kt + 1)
            less(xlo[:, kt, :], ps[:, kt % 8, :], xhi[:, kt, :]).then_inc(xT_lo, 1)
        split(G_POOL, 0, 0, 0)
        ve.wait_ge(gate_ps, 1)
        ve.wait_ge(par_in, 64)
        for t in range(TT):
            V.tensor_tensor(gate_pre[:, t, :], X[0][:, t * NG:(t + 1) * NG], bias_if[:, :], ALU.add)\
                .then_inc(pre_rdy, 1)
        f_gates = gate_pre[:, :, :].rearrange("p t (d k h) -> p t d k h", d=2, k=2)[:, :, :, 1, :]
        ve.wait_ge(soft_rdy, 1)
        ve.wait_ge(pre_rdy, TT)
        for d in range(2):
            last = V.scalar_tensor_tensor(f_gates[:, :, d, :], f_gates[:, :, d, :], 0.0, gate_tmp[:, 2, :, d, :],
                                          ALU.min, ALU.subtract)
            if d == 0:
                order.add(last)
        last.then_inc(gate_rdy, 1)
        ve.wait_ge(xT_ps, KT)
        order.add(V.memset(g_ones[0:HEADS, :], 1.0))

        def scans():
            fwd, bwd = slice(None), slice(None, None, -1)
            ve.wait_ge(rows_ps, 1)
            order.wait()
            for d, way in ((0, fwd), (1, bwd)):
                order.add(V.tensor_tensor_scan(g_f[0:HEADS, d, way], g_ones[0:HEADS, :], X[2 * d + 1][0:HEADS, way],
                                               0.0, ALU.mult, ALU.add))
            order.wait()
            for d in range(2):
                order.add(V.tensor_tensor(g_a[0:HEADS, d, :], X[2 * d][0:HEADS, :], g_f[0:HEADS, d, :],
                                          ALU.subtract))
            order.wait()
            for d, way in ((0, fwd), (1, bwd)):
                order.add(V.tensor_tensor_scan(g_m[0:HEADS, d, way], g_a[0:HEADS, d, way], g_a[0:HEADS, d, way],
                                               0.0, ALU.max, ALU.max))
            order.wait()
            V.tensor_scalar(g_neg[0:HEADS, :, :], g_m[0:HEADS, :, :], -1.0, None, ALU.mult).then_inc(neg_rdy, 1)
            ve.wait_ge(neg_rdy, 1)
            V.tensor_tensor(g_m[0:HEADS, :, :], g_m[0:HEADS, :, :], g_f[0:HEADS, :, :], ALU.add).then_inc(m_rdy, 1)

        def columns():
            ve.wait_ge(col_ps, 1)
            cols = X[0][:, 0:4 * TT * HEADS].rearrange("p (k d t h) -> p k h d t", k=2, d=2, t=TT)
            V.tensor_copy(a_col[:, :, :, :], cols[:, 0]).then_inc(col_rdy, 1)
            V.tensor_copy(em_col[:, :, :, :], cols[:, 1]).then_inc(col_rdy, 1)

        def group_weights(j):
            ve.wait_ge(grph, j + 1)
            less(grp_lo[:, :], grp_raw[:, j, :], grp_hi[:, :]).then_inc(grpl, 1)

        def differences(j):
            ve.wait_ge(unit_out, 4 * j + 4)
            ve.wait_ge(consts, 5)
            for gg in range(2):
                w, win = 2 * j + gg, WINDOWS[2 * j + gg]
                u = pool_u[:, 2 * gg:2 * gg + 2, :]
                src, bufs, lo, hi, step = u, [sum_a, sum_b], 1, S + 2 * PAD, 1
                order.wait()
                order.add(V.tensor_tensor(sum_a[:, :, 1:hi], u[:, :, 0:hi - 1], u[:, :, 1:hi], ALU.add))
                src, width, n = sum_a, 2, 1
                while width < win:
                    step = width // 2
                    lo, hi = lo + step, hi - step
                    dst = bufs[n % 2]
                    order.wait()
                    order.add(V.tensor_tensor(dst[:, :, lo:hi], src[:, :, lo - step:hi - step],
                                              src[:, :, lo + step:hi + step], ALU.add))
                    src, width, n = dst, 2 * width, n + 1
                order.wait()
                h = win // 2
                if h > 0:
                    for edge, at in ((0, PAD), (PAD, S)):
                        sl = src[:, :, at:at + PAD]
                        order.add(V.scalar_tensor_tensor(
                            sl, sl, float(win), redge[:, w:w + 1, edge:edge + PAD].to_broadcast((P, 2, PAD)),
                            ALU.mult, ALU.mult))
                order.wait()
                V.scalar_tensor_tensor(src[:, :, PAD:PAD + S], src[:, :, PAD:PAD + S], 1.0 / win,
                                       u[:, :, PAD:PAD + S], ALU.mult, ALU.subtract).then_inc(diff_rdy, 1)
                ve.wait_ge(dhi_rdy, w + 1)
                less(dlo[:, 2 * gg:2 * gg + 2, :], src[:, :, PAD:PAD + S], dhi[:, 2 * gg:2 * gg + 2, :])\
                    .then_inc(dlo_rdy, 1)
                ve.wait_ge(dlo_rdy, w + 1)

        def groups_out(j):
            for n in range(4):
                k = 4 * j + n
                ve.wait_ge(pm_hi, k + 1)
                V.scalar_tensor_tensor(pmlo(k), X[n], ps_col[:, k:k + 1], pmhi[:, k, :].bitcast(F32), ALU.mult,
                                       ALU.subtract).then_inc(pm_lo, 1)

        for k in range(8):
            split(G_POOL, 0, 0, k + 1)
            if k == 4:
                scans()
                group_weights(0)
            if k == 5:
                differences(0)
            if k == 6:
                columns()
            if k == 7:
                groups_out(0)
                group_weights(1)
        differences(1)
        groups_out(1)

        with ve.Fori(0, NCH // 2) as i:
            for k in range(12):
                split(G_A, i, 12, k + 1)
                if k % 6 == 5:
                    j = k // 6
                    ve.wait_ge(zt_free, 2 * i + j + 1)
                    for n in range(4):
                        ve.wait_ge(sub_done, 48 * i + (4 * (G_A + k) + n + 1))
                        if n == 0:
                            ve.wait_ge(unit_out, 16 * i + 4 * (U_A + 2 * j + 1))
                        V.tensor_tensor(zt[:, n, :], U[n], sgp[:, n, :], ALU.mult).then_inc(unit_out, 1)

        def decayed_scores(i, h):
            ve.wait_ge(e_rdy, 28 * i + 14 * h + 14)
            for kt in range(TT):
                ve.wait_ge(s_ps, 8 * i + 4 * h + kt + 1)
                for d, off, (at, n) in ((0, F_OFF[kt], f_range(kt)), (1, B_OFF[kt], b_range(kt))):
                    a = amat[h][:, d, off:off + n]
                    V.scalar_tensor_tensor(a, X[kt][:, at:at + n], HD ** -0.5, a, ALU.mult, ALU.mult)\
                        .then_inc(a_rdy, 1)

        def reciprocals(i, h, d):
            em = em_col[:, bass.ds(2 * i + h, 1), d, :].rearrange("p a t -> p (a t)")
            ve.wait_ge(den_abs, 4 * i + 2 * h + d + 1)
            order.add(V.tensor_tensor(den[:, d, :], den[:, d, :], em, ALU.max))
            order.wait()
            V.reciprocal(den[:, d, :], den[:, d, :]).then_inc(rec_rdy, 1)

        def backward_and_norm(i, h):
            reciprocals(i, h, 1)
            ve.wait_ge(rec_rdy, 4 * i + 2 * h + 2)
            ve.wait_ge(hf_rdy, 8 * i + 4 * h + 4)
            for t in range(TT):
                o = hh[h][:, t, :]
                order.add(V.scalar_tensor_tensor(o, X[t][:, 0:HD], den[:, 1, t:t + 1], o, ALU.mult, ALU.add))
            order.wait()
            for t in range(TT):
                order.add(V.bn_stats(stat[:, t, 0, :], hh[h][:, t, :]))
            order.wait()
            order.add(V.memset(carrier[:, :], 0.0))
            for t in range(TT):
                last_ = V.bn_aggr(mv[:, t, :], stat[:, t, 0, :])
                if t < TT - 1:
                    order.add(last_)
            last_.then_inc(var_rdy, 1)
            order.wait()
            ve.wait_ge(sq_rdy, 2 * i + h + 1)
            order.add(V.reciprocal(rstd[:, :], rstd[:, :]))
            order.wait()
            for t in range(TT):
                V.tensor_scalar(hh[h][:, t, :], hh[h][:, t, :], mv[:, t, 0:1], rstd[:, t:t + 1], ALU.subtract,
                                ALU.mult).then_inc(hn_rdy, 1)

        def gated_head(i, h):
            for c in range(2):
                n = 2 * h + c
                ve.wait_ge(ht_ps, 4 * i + n + 1)
                nw = nw_col[:, bass.ds(4 * i + n, 1)]
                V.scalar_tensor_tensor(so[:, n, :], X[c], nw, so[:, n, :], ALU.mult, ALU.mult).then_inc(hg_rdy, 1)

        with ve.Fori(0, PAIRS) as i:
            order.loop(i, 30)
            for k in range(20):
                split(G_B, i, 20, k + 1)
                if k == 9:
                    decayed_scores(i, 0)
                if k == 11:
                    decayed_scores(i, 1)
                if k == 13:
                    reciprocals(i, 0, 0)
                if k == 14:
                    backward_and_norm(i, 0)
                if k == 15:
                    ve.wait_ge(hf_rdy, 8 * i + 4)
                    reciprocals(i, 1, 0)
                if k == 16:
                    ve.wait_ge(hn_rdy, 8 * i + 4)
                    backward_and_norm(i, 1)
                if k == 17:
                    ve.wait_ge(unit_out, 20 * i + 4 * (U_B + 4))
                    gated_head(i, 0)
                if k == 18:
                    gated_head(i, 1)
            order.end(PAIRS)
        for c in range(NCH):
            ve.wait_ge(hgs_hi, c + 1)
            less(hglo[:, 4 * c:4 * c + 4, :], hraw[:, c, :, :], hghi[:, 4 * c:4 * c + 4, :]).then_inc(hgs_lo, 1)
        with ve.Fori(0, NCH) as i:
            order.loop(i, 0)
            for k in range(4):
                split(G_C, i, 4, k + 1)
                if k == 3:
                    for n in range(4):
                        ve.wait_ge(cz_in[n % 2], 64 * i + 32 * (n // 2) + 32)
                        ve.wait_ge(sub_done, 16 * i + (4 * (G_C + k) + n + 1))
                        V.tensor_tensor(cz[:, n % 2, 0, :], U[n], cz[:, n % 2, 0, :], ALU.mult)\
                            .then_inc(unit_out, 1)
                        ve.wait_ge(unit_out, 4 * i + (4 * U_C + n + 1))
                        V.tensor_tensor(cz[:, n % 2, 1, :], cz[:, n % 2, 0, :], cz[:, n % 2, 1, :], ALU.add)\
                            .then_inc(z_rdy, 1)
                        ve.wait_ge(z_hi, 4 * i + n + 1)
                        row = bass.ds(4 * i + n, 1)
                        less(zlo[:, row, :], cz[:, n % 2, 1:2, :], zhi[:, row, :]).then_inc(z_lo, 1)
            order.end(NCH)

        def residual(i):
            ve.wait_ge(xc_in, 16 * i + 16)
            for t in range(TT):
                ve.wait_ge(sub_done, 16 * i + (4 * (G_D + 3) + t + 1))
                o = acc[:, t, bass.ds(i * CW, CW)]
                V.scalar_tensor_tensor(o, xc[:, t, :], ALPHA, U[t], ALU.mult, ALU.add).then_inc(unit_out, 1)
            for t in range(TT):
                ve.wait_ge(unit_out, 4 * i + (4 * U_D + t + 1))
                order.add(V.bn_stats(stat[:, t, bass.ds(i, 1), :].rearrange("p a b -> p (a b)"),
                                     acc[:, t, bass.ds(i * CW, CW)]))

        with ve.Fori(0, NCH - 1) as i:
            order.loop(i, TT)
            for k in range(4):
                split(G_D, i, 4, k + 1)
            residual(i)
            order.end(NCH - 1)
        for k in range(3):
            split(G_D + 4 * (NCH - 1), 0, 0, k + 1)
        residual(NCH - 1)

        def norm_scale(var_sem, sq_sem, out_sem):
            order.wait()
            for t in range(TT):
                last_ = V.bn_aggr(mv[:, t, :], stat[:, t, :, :].rearrange("p a b -> p (a b)"))
                if t < TT - 1:
                    order.add(last_)
            last_.then_inc(var_sem, 1)
            order.wait()
            ve.wait_ge(sq_sem, 1)
            order.add(V.reciprocal(rstd[:, :], rstd[:, :]))
            order.wait()
            V.scalar_tensor_tensor(nmr[:, :], mv[:, :, 0], -1.0, rstd[:, :], ALU.mult, ALU.mult)\
                .then_inc(out_sem, 1)

        norm_scale(var1_rdy, sq1_rdy, rst_rdy)
        ve.wait_ge(ln_in, 32)

        def norm_affine(t, nrm_sem, g, b, done):
            ve.wait_ge(nrm_sem, t + 1)
            order.add(V.tensor_tensor(acc[:, t, :], acc[:, t, :], g[:, :], ALU.mult))
            order.wait()
            V.tensor_tensor(acc[:, t, :], acc[:, t, :], b[:, :], ALU.add).then_inc(done, 1)

        def affinities(t):
            ve.wait_ge(lg_ps, t + 1)
            if t:
                ve.wait_ge(lg_exp, t)
                ve.wait_ge(aff_rdy, t)
            V.reduce_max(sm_max[:, :], ps[:, 4 * (t % 2), 0:NE], AX.X, negate=True).then_inc(lg_max, 1)
            ve.wait_ge(lg_exp, t + 1)
            order.add(V.reciprocal(sm_rec[:, :], sm_sum[:, :]))
            order.wait()
            V.tensor_scalar(aff_c[:, t, :], sm_exp[:, :], sm_rec[:, 0:1], None, ALU.mult).then_inc(aff_rdy, 1)

        norm_affine(0, ln_nrm, lng1, lnb1, x1_rdy)
        norm_affine(1, ln_nrm, lng1, lnb1, x1_rdy)
        affinities(0)
        norm_affine(2, ln_nrm, lng1, lnb1, x1_rdy)
        affinities(1)
        norm_affine(3, ln_nrm, lng1, lnb1, x1_rdy)
        affinities(2)
        affinities(3)
        order.add(V.memset(r_ones[0:NE, :], 1.0))
        ve.wait_ge(affT_ps, 1)
        order.add(V.tensor_copy(aff_r[0:NE, :], X[1][0:NE, :]))
        now = aff_r
        for r in range(CAP // 8):
            order.wait()
            order.add(V.max(top8[0:NE, :], now[0:NE, :]))
            order.wait()
            order.add(V.match_replace(work[r % 2][0:NE, :], top8[0:NE, :], now[0:NE, :], -1.0))
            now = work[r % 2]
        order.wait()
        order.add(V.tensor_tensor(picked[0:NE, :], aff_r[0:NE, :], now[0:NE, :], ALU.not_equal))
        order.wait()
        order.add(V.tensor_tensor_scan(slot_r[0:NE, :], r_ones[0:NE, :], picked[0:NE, :], 0.0, ALU.mult, ALU.add))
        order.wait()
        order.add(V.tensor_tensor(slot_r[0:NE, :], slot_r[0:NE, :], picked[0:NE, :], ALU.mult))
        order.wait()
        V.tensor_scalar(slot_r[0:NE, :], slot_r[0:NE, :], -1.0, None, ALU.add).then_inc(slot_rdy, 1)
        ve.wait_ge(slotT_ps, 1)
        order.add(V.tensor_copy(slot_c[:, :, :].rearrange("p t e -> p (t e)"), X[0][:, 0:TT * NE]))
        order.wait()

        def one_hots(q):
            for e in range(2):
                for t in range(TT):
                    V.tensor_scalar(onehot[:, e, t, :], slot_no[:, :], slot_c[:, t, bass.ds(2 * q + e, 1)], None,
                                    ALU.is_equal).then_inc(oh_rdy, 1)

        def token_numbers(q):
            ve.wait_ge(tok_ps, q + 1)
            V.tensor_copy(tok_f[:, :], X[2][:, 0:1]).then_inc(tok_cp, 1)
            ve.wait_ge(tok_cp, q + 1)
            V.tensor_copy(tok_u[:, :], tok_f[:, :]).then_inc(tok_rdy, 1)

        def tokens_lo(q):
            for b in range(4):
                ve.wait_ge(xeT_hi, 4 * q + b + 1)
                less(xeT[:, 4 * b:4 * b + 4, :, CAP:P], X[b].rearrange("p (r e n) -> p r e n", r=4, e=2),
                     xeT[:, 4 * b:4 * b + 4, :, 0:CAP]).then_inc(xeT_lo, 1)

        def hidden(q, e):
            ve.wait_ge(sig_rdy, 2 * q + e + 1)
            V.tensor_tensor(hid_tmp[:, :], X[0], hid_tmp[:, :], ALU.mult).then_inc(silu_rdy, 1)
            ve.wait_ge(silu_rdy, 2 * q + e + 1)
            ve.wait_ge(guT_ps, 4 * q + 2 * e + 2)
            V.tensor_tensor(hid_tmp[:, :], X[1], hid_tmp[:, :], ALU.mult).then_inc(hid_pre, 1)
            ve.wait_ge(hid_hi, 2 * q + e + 1)
            less(hid[e][:, :, CAP:P], hid_tmp[:, :].rearrange("p (f n) -> p f n", f=FT),
                 hid[e][:, :, 0:CAP]).then_inc(hid_lo, 1)

        def accumulate(q, c):
            ve.wait_ge(comb_ps, 16 * q + 4 * c + 4 + 1)
            o = acc[:, :, c * CW:(c + 1) * CW]
            V.tensor_tensor(o, Xall, o, ALU.add).then_inc(acc_add, 1)

        def split_m(q, k):
            ve.wait_ge(hi_done, 48 * q + (G_END + k + 1))
            less(wlo_m[k % HL_M][:, :, :].rearrange("p k n -> p (k n)"), raw_m[k % RAW_M][:, :],
                 whi_m[k % HL_M][:, :, :].rearrange("p k n -> p (k n)")).then_inc(lo_done, 1)

        def expert_pair(q, last_pair):
            for k in range(AHEAD_M):
                split_m(q, k)
            for k in range(48):
                if k + AHEAD_M < 48:
                    split_m(q, k + AHEAD_M)
                if k == 1:
                    ve.wait_ge(gw_ps, q + 1)
                    V.tensor_copy(gate_w[:, :], X[3][:, 0:2]).then_inc(gw_rdy, 1)
                if k == 17:
                    hidden(q, 0)
                if k == 18 and not last_pair:
                    one_hots(q + 1)
                if k == 20 and not last_pair:
                    token_numbers(q + 1)
                if k == 33:
                    hidden(q, 1)
                if k >= 32 and k % 2 == 1:
                    c, e = (k - 32) // 4, (k - 32) % 4 // 2
                    ve.wait_ge(y_hi, 8 * q + 2 * c + e + 1)
                    V.scalar_tensor_tensor(ylo[:, e, :], U[2 * e + c % 2], gate_w[:, e:e + 1],
                                           yhi[:, e, :].bitcast(F32), ALU.mult, ALU.subtract).then_inc(y_lo, 1)
                if k in (37, 41, 45):
                    accumulate(q, (k - 37) // 4)
                if k == 46 and not last_pair:
                    tokens_lo(q + 1)
            accumulate(q, 3)

        one_hots(0)
        token_numbers(0)
        tokens_lo(0)
        ve.wait_ge(acc_scaled, TT)
        with ve.Fori(0, EP - 1) as i:
            expert_pair(i, False)
        expert_pair(EP - 1, True)
        ve.wait_ge(acc_add, 4 * EP + 1)
        for t in range(TT):
            for c in range(NCH):
                order.add(V.bn_stats(stat[:, t, c, :], acc[:, t, c * CW:(c + 1) * CW]))
        norm_scale(o_var, o_sq, o_rst)
        ve.wait_ge(ln2_in, 32)
        for t in range(TT):
            norm_affine(t, o_nrm, lng2, lnb2, o_rdy)

    keep.close()


_INS = ["x", "w_in", "b_if", "w_pool_grp", "pool_scale", "w_pool_up", "mlstm_norm_w", "w_mlstm_up", "w_out",
        "ln1_g", "ln1_b", "w_router", "w_gate", "w_up", "w_down", "ln2_g", "ln2_b"]


def kernel(**inputs):
    import concourse.bacc as bacc
    import numpy as np
    from concourse.bass_utils import run_bass_kernel_spmd

    nc = bacc.Bacc("TRN2", target_bir_lowering=False, num_devices=1)
    arrays, args = {}, []
    for name in _INS:
        a = np.ascontiguousarray(inputs[name])
        arrays[f"in_{name}"] = a
        args.append(nc.dram_tensor(f"in_{name}", a.shape, mybir.dt.from_np(a.dtype), kind="ExternalInput").ap())
    args.append(nc.dram_tensor("out_x", (1, S, D), F32, kind="ExternalOutput").ap())
    build(nc, args)
    r = run_bass_kernel_spmd(nc, [arrays], core_ids=[0])
    return r.results[0]["out_x"]
```

```python
from contextlib import ExitStack

import concourse.bass as bass
from concourse import mybir
from concourse.alu_op_type import AluOpType as ALU

F32 = mybir.dt.float32
F32R = mybir.dt.float32r
U32 = mybir.dt.uint32
ACT = mybir.ActivationFunctionType
AX = mybir.AxisListType

P = 128
S = 512
D = 2048
TT = S // P
KT = D // P
CW = 512
SK = 4
NCH = D // CW
PW = D // 2
WINDOWS = (2, 4, 8, 16)
GD = PW // len(WINDOWS)
PAD = max(WINDOWS) // 2
HEADS = 8
HD = D // HEADS
PAIRS = HEADS // 2
NE = 16
CAP = 2 * S // NE
FF = D // 2
FT = FF // P
EP = NE // 2
COL_Q = PW
COL_K = COL_Q + D
COL_V = COL_K + D
COL_O = COL_V + D
COL_IF = COL_O + D
NG = 4 * HEADS
COL_GP = COL_IF + NG
COL_GM = COL_GP + D
ALPHA = 2.0 ** 0.25
LN_EPS = 1e-5
GN_EPS = 1e-6
NEG = -1e30

RAW = 2
HL = 2
RAW_M = 8
HL_M = 3
AHEAD_M = HL_M - 1

G_POOL = 0
G_A = G_POOL + 2 * 4
G_B = G_A + NCH * (4 + 2)
G_C = G_B + PAIRS * 5 * 4
G_D = G_C + NCH * 4
G_END = G_D + NCH * 4
U_POOL = 0
U_A = 2
U_B = U_A + 2 * NCH
U_C = U_B + 5 * PAIRS
U_D = U_C + NCH

F_OFF = [0, 512, 896, 1152]
B_OFF = [0, 128, 384, 768]
TRI = 1280


def f_range(i):
    return P * i, S - P * i


def b_range(i):
    return 0, P * (i + 1)


class Order:

    def __init__(self, eng, sem):
        self.eng, self.sem, self.n, self.turn = eng, sem, 0, 0

    def add(self, ins):
        ins.then_inc(self.sem, 1)
        self.n += 1

    def wait(self):
        self.eng.wait_ge(self.sem, self.turn + self.n)

    def loop(self, i, per):
        self.start, self.per, self.turn = self.n, per, i * per

    def end(self, trips):
        assert self.n - self.start == self.per, (self.n - self.start, self.per)
        self.n, self.turn = self.start + self.per * trips, 0


def build(nc, io):
    (x, w_in, b_if, w_pool_grp, pool_scale, w_pool_up, mlstm_norm_w, w_mlstm_up, w_out, ln1_g, ln1_b,
     w_router, w_gate, w_up, w_down, ln2_g, ln2_b, out) = io

    def dram(name, shape):
        return nc.dram_tensor(name, shape, F32, kind="Internal").ap()

    gate_rows_d = dram("gate_rows_d", (2, HEADS, S))
    zp_d = dram("zp_d", (D, S))
    sgm_d = dram("sgm_d", (D, S))
    hg_d = dram("hg_d", (D, S))
    x1_d = dram("x1_d", (S, D))

    def tiles_of_rows(w):
        return w.rearrange("(k p) n -> p k n", p=P)

    w_in_v, pool_up_v = tiles_of_rows(w_in[0]), tiles_of_rows(w_pool_up[0])
    mlstm_up_v, w_out_v = tiles_of_rows(w_mlstm_up[0]), tiles_of_rows(w_out[0])
    zp_v, sgm_v, hg_v = tiles_of_rows(zp_d), tiles_of_rows(sgm_d), tiles_of_rows(hg_d)
    x_v, out_v = tiles_of_rows(x[0]), tiles_of_rows(out[0])
    gate_v = w_gate[0].rearrange("e (k p) n -> p e k n", p=P)
    up_v = w_up[0].rearrange("e (k p) n -> p e k n", p=P)
    down_v = w_down[0].rearrange("e (k p) n -> p e k n", p=P)

    keep = ExitStack()
    keep.__enter__()

    def on(stack, name, shape, dt=F32):
        return stack.enter_context(nc.sbuf_tensor(name, [P, *shape], dt))

    def sb(name, shape, dt=F32):
        return on(keep, name, shape, dt)

    raw = [sb(f"raw{n}", [SK * CW]) for n in range(RAW)]
    whi = [sb(f"whi{n}", [SK, CW], F32R) for n in range(HL)]
    wlo = [sb(f"wlo{n}", [SK, CW], F32R) for n in range(HL)]
    ident = sb("ident", [P])
    halves = sb("halves", [CAP])
    slot_no = sb("slot_no", [P])
    behind = sb("behind", [2, P])
    token_no = sb("token_no", [TT])
    bias_if = sb("bias_if", [1])
    a_col = sb("a_col", [HEADS, 2, TT])
    em_col = sb("em_col", [HEADS, 2, TT])
    nw_col = sb("nw_col", [KT])
    ps_col = sb("ps_col", [PW // P])
    den = sb("den", [2, TT])
    stat = sb("stat", [TT, NCH, 6])
    mv = sb("mv", [TT, 2])
    rstd = sb("rstd", [TT])
    geps = sb("geps", [1])
    leps = sb("leps", [1])
    carrier = sb("carrier", [1])
    v_one = sb("v_one", [4 * TT])
    credit = sb("credit", [8])
    part = ExitStack()
    xhi = on(part, "xhi", [KT, S], F32R)
    xlo = on(part, "xlo", [KT, S], F32R)
    sub = ExitStack()
    xst = on(sub, "xst", [NCH, TT, CW])
    wif = on(sub, "wif", [KT, NG])
    wif_hi = on(sub, "wif_hi", [KT, NG], F32R)
    wif_lo = on(sub, "wif_lo", [KT, NG], F32R)
    sub.close()
    g_ones = on(sub, "g_ones", [S])
    g_f = on(sub, "g_f", [2, S])
    g_a = on(sub, "g_a", [2, S])
    g_m = on(sub, "g_m", [2, S])
    g_em = on(sub, "g_em", [2, S])
    g_neg = on(sub, "g_neg", [2, S])
    gate_pre, gate_log = g_neg[0:NG, 0, :], g_neg[0:NG, 1, :]
    sub.close()
    pmhi = on(sub, "pmhi", [PW // P, S], F32R)
    pmlo_a = on(sub, "pmlo_a", [PW // P // 2, S], F32R)
    late = ExitStack()
    grp_raw = on(late, "grp_raw", [2, 4 * GD])
    late.close()
    pmlo_b = on(sub, "pmlo_b", [PW // P // 2, S], F32R)
    late = ExitStack()
    dhi = on(late, "dhi", [4, S], F32R)
    dlo = on(late, "dlo", [4, S], F32R)
    pool_u = on(late, "pool_u", [4, S + 2 * PAD])
    sum_a = on(late, "sum_a", [2, S + 2 * PAD])
    sum_b = on(late, "sum_b", [2, S + 2 * PAD])
    redge = on(late, "redge", [len(WINDOWS), 2 * PAD])
    grp_hi = on(late, "grp_hi", [4 * GD], F32R)
    grp_lo = on(late, "grp_lo", [4 * GD], F32R)
    late.close()
    sgp = on(late, "sgp", [4, S])
    zt = on(late, "zt", [4, S])
    late.close()
    sub.close()
    v_hi = on(sub, "v_hi", [TT, 2, HD + 2], F32R)
    v_lo = on(sub, "v_lo", [TT, 2, HD + 2], F32R)
    amat = on(sub, "amat", [2, TRI])
    a_hi = on(sub, "a_hi", [2, TRI], F32R)
    a_lo = on(sub, "a_lo", [2, TRI], F32R)
    k_lo = on(late, "k_lo", [4, S], F32R)
    late.close()
    hh = [on(sub, f"hh{h}", [TT, HD]) for h in range(2)]
    q_lo = on(sub, "q_lo", [4, S], F32R)
    k_hi = on(late, "k_hi", [4, S], F32R)
    q_hi = on(late, "q_hi", [4, S], F32R)
    late.close()
    sgm = on(sub, "sgm", [4, S])
    so = on(sub, "so", [4, S])
    gb = on(sub, "gb", [2, S])
    gd = on(sub, "gd", [2, S])
    sub.close()
    part.close()
    hghi = on(part, "hghi", [KT, S], F32R)
    hglo = on(part, "hglo", [KT, S], F32R)
    hraw = on(sub, "hraw", [NCH, 4, S])
    sub.close()
    zhi = on(sub, "zhi", [KT, S], F32R)
    zlo = on(sub, "zlo", [KT, S], F32R)
    late = ExitStack()
    cz = on(late, "cz", [2, 2, S])
    late.close()
    xc = on(late, "xc", [TT, CW])
    late.close()
    sub.close()
    part.close()
    acc = on(part, "acc", [TT, D])
    raw_new = [on(part, f"raw{n}", [SK * CW]) for n in range(RAW, RAW + 2)]
    lng1 = on(sub, "lng1", [D])
    lnb1 = on(sub, "lnb1", [D])
    sub.close()
    whi_m = [on(part, "whi2", [SK, CW], F32R)] + whi
    wlo_m = [on(part, "wlo2", [SK, CW], F32R)] + wlo
    slot_c = on(part, "slot_c", [TT, NE])
    aff_c = on(part, "aff_c", [TT, NE])
    raw_new += [on(part, f"raw{n}", [SK * CW]) for n in range(RAW + 2, RAW_M)]
    raw_m = raw_new + raw
    x1T = [on(sub, f"x1T{n}", [KT, P]) for n in range(2)]
    wr = on(sub, "wr", [KT, NE])
    lgT = on(sub, "lgT", [S])
    sm_max = on(sub, "sm_max", [TT, 1])
    sm_sum = on(sub, "sm_sum", [TT, 1])
    sm_exp = on(sub, "sm_exp", [TT, NE])
    aff_r = on(sub, "aff_r", [S])
    work = [on(sub, f"work{n}", [S]) for n in range(2)]
    top8 = on(sub, "top8", [8])
    picked = on(sub, "picked", [S])
    slot_r = on(sub, "slot_r", [S])
    r_ones = on(sub, "r_ones", [S])
    sub.close()
    xe = on(part, "xe", [D])
    xeT = on(late, "xeT", [KT, 2, P], F32R)
    late.close()
    lng2 = on(part, "lng2", [D])
    lnb2 = on(part, "lnb2", [D])
    gu = on(late, "gu", [2, FF])
    late.close()
    yhi1 = on(part, "yhi1", [2, CW], F32R)
    ylo1 = on(part, "ylo1", [2, CW], F32R)
    onehot = on(part, "onehot", [2, TT, P])
    scat = on(part, "scat", [2, S], F32R)
    gate_w = on(part, "gate_w", [2])
    tok_f = on(part, "tok_f", [1])
    tok_u = on(part, "tok_u", [1], U32)
    hid_tmp = on(part, "hid_tmp", [CW])
    hid = [on(part, f"hid{e}", [FT, P], F32R) for e in range(2)]
    yhi = [on(part, "yhi0", [2, CW], F32R), yhi1]
    ylo = [on(part, "ylo0", [2, CW], F32R), ylo1]
    part.close()

    def pmlo(k):
        half = PW // P // 2
        return (pmlo_a if k < half else pmlo_b)[:, k % half, :]

    ps = keep.enter_context(nc.psum_tensor("ps", [P, 8, CW], F32))
    U = [ps[:, n, :] for n in range(4)]
    X = [ps[:, 4 + n, :] for n in range(4)]
    Xall = ps[:, 4:8, :]

    def sem(name):
        return keep.enter_context(nc.semaphore(name))

    raw_in = [sem(f"raw_in{n}") for n in range(RAW)]
    raw_in_m = [sem(f"raw_in_m{n}") for n in range(RAW_M)]
    hi_done = sem("hi_done")
    lo_done = sem("lo_done")
    sub_done = sem("sub_done")
    unit_out = sem("unit_out")
    consts = sem("consts")
    x_in = [sem(f"x_in{n}") for n in range(NCH)]
    wif_in, par_in = sem("wif_in"), sem("par_in")
    id_rdy = sem("id_rdy")
    xT_ps, xT_hi, xT_lo = sem("xT_ps"), sem("xT_hi"), sem("xT_lo")
    wif_h, wif_l = sem("wif_h"), sem("wif_l")
    gate_ps, pre_rdy, soft_rdy, gate_rdy = sem("gate_ps"), sem("pre_rdy"), sem("soft_rdy"), sem("gate_rdy")
    rows_ps, neg_rdy, m_rdy, em_rdy = sem("rows_ps"), sem("neg_rdy"), sem("m_rdy"), sem("em_rdy")
    neg_st, col_ps, col_rdy = sem("neg_st"), sem("col_ps"), sem("col_rdy")
    grp_in, grph, grpl, grp_ps = sem("grp_in"), sem("grph"), sem("grpl"), sem("grp_ps")
    diff_rdy, dhi_rdy, dlo_rdy = sem("diff_rdy"), sem("dhi_rdy"), sem("dlo_rdy")
    pm_hi, pm_lo = sem("pm_hi"), sem("pm_lo")
    zp_st = sem("zp_st")
    zt_free, so_free, sgm_free = sem("zt_free"), sem("so_free"), sem("sgm_free")
    v_ones, kqv_hi, a_hi_rdy, a_lo_rdy = sem("v_ones"), sem("kqv_hi"), sem("a_hi_rdy"), sem("a_lo_rdy")
    gb_in, gd_rdy, e_rdy, s_ps, a_rdy = sem("gb_in"), sem("gd_rdy"), sem("e_rdy"), sem("s_ps"), sem("a_rdy")
    av_ps, den_abs, rec_rdy, hf_rdy = sem("av_ps"), sem("den_abs"), sem("rec_rdy"), sem("hf_rdy")
    var_rdy, sq_rdy, hn_rdy = sem("var_rdy"), sem("sq_rdy"), sem("hn_rdy")
    ht_ps, hg_rdy, hg_st, sgm_st = sem("ht_ps"), sem("hg_rdy"), sem("hg_st"), sem("sgm_st")
    hraw_in = [sem(f"hraw_in{n}") for n in range(NCH)]
    hgs_hi, hgs_lo = sem("hgs_hi"), sem("hgs_lo")
    cz_in = [sem(f"cz_in{n}") for n in range(2)]
    z_rdy, z_hi, z_lo = sem("z_rdy"), sem("z_hi"), sem("z_lo")
    xc_in = sem("xc_in")
    dve, act, pool = sem("dve"), sem("act"), sem("pool")
    var1_rdy, sq1_rdy, x1_rdy, x1_st = sem("var1_rdy"), sem("sq1_rdy"), sem("x1_rdy"), sem("x1_st")
    ln_in, ln2_in = sem("ln_in"), sem("ln2_in")
    wr_in, x1T_ps, x1T_rdy = sem("wr_in"), sem("x1T_ps"), sem("x1T_rdy")
    lg_ps, lgT_rdy, lg_max, lg_exp, aff_rdy = (sem("lg_ps"), sem("lgT_rdy"), sem("lg_max"), sem("lg_exp"),
                                               sem("aff_rdy"))
    affT_ps, slot_rdy, slotT_ps, acc_scaled = sem("affT_ps"), sem("slot_rdy"), sem("slotT_ps"), sem("acc_scaled")
    oh_rdy, tok_ps, tok_cp, tok_rdy = sem("oh_rdy"), sem("tok_ps"), sem("tok_cp"), sem("tok_rdy")
    xe_in, xeT_ps, xeT_hi, xeT_lo = sem("xe_in"), sem("xeT_ps"), sem("xeT_hi"), sem("xeT_lo")
    scat_ps, scat_rdy, gw_ps, gw_rdy = sem("scat_ps"), sem("scat_rdy"), sem("gw_ps"), sem("gw_rdy")
    slots_free = sem("slots_free")
    gu_rdy, guT_ps, sig_rdy, silu_rdy, hid_pre = (sem("gu_rdy"), sem("guT_ps"), sem("sig_rdy"), sem("silu_rdy"),
                                                  sem("hid_pre"))
    hid_hi, hid_lo, y_hi, y_lo = sem("hid_hi"), sem("hid_lo"), sem("y_hi"), sem("y_lo")
    comb_ps, acc_add = sem("comb_ps"), sem("acc_add")
    o_var, o_sq, o_rdy, out_st = sem("o_var"), sem("o_sq"), sem("o_rdy"), sem("out_st")

    ahead = [zt_free, so_free, sgm_free, hg_rdy, hid_lo, y_lo, comb_ps, acc_add]

    class WaitTaker:

        def __init__(self, eng):
            self.eng, self.reg = eng, eng.alloc_register("count")
            eng.reg_mov(self.reg, 0)

        def take_wait(self):
            self.eng.reg_add(self.reg, self.reg, 1)
            self.eng.reg_add(self.reg, self.reg, 1)

    block = keep.enter_context(nc.Block())

    @block.sync
    def _(sp):
        def load_stage(base, i, per, k, src):
            if base + k >= RAW:
                sp.wait_ge(lo_done, i * per + (base + k - RAW + 1))
            sp.dma_start(raw[k % RAW][:, :].rearrange("p (k n) -> p k n", k=SK), src).then_inc(raw_in[k % RAW], 16)

        for c in range(NCH):
            sp.dma_start(xst[:, c, :, :], x_v[:, :, c * CW:(c + 1) * CW]).then_inc(x_in[c], 16)
        for k in range(8):
            u, s = k // 4, k % 4
            load_stage(G_POOL, 0, 0, k, w_in_v[:, SK * s:SK * s + SK, u * CW:(u + 1) * CW])
        with sp.Fori(1, NCH // 2 + 1) as after:
            i = after - 1
            for j in range(2):
                for s in range(4):
                    load_stage(G_A, i, 12, 6 * j + s,
                               w_in_v[:, SK * s:SK * s + SK, bass.ds(i * (2 * CW) + (COL_GP + j * CW), CW)])
                for s in range(2):
                    load_stage(G_A, i, 12, 6 * j + 4 + s,
                               pool_up_v[:, SK * s:SK * s + SK, bass.ds(after * (2 * CW) + (j - 2) * CW, CW)])
        with sp.Fori(0, PAIRS) as i:
            for n, col in enumerate((COL_K, COL_Q, COL_V, COL_O, COL_GM)):
                for s in range(4):
                    load_stage(G_B, i, 20, 4 * n + s, w_in_v[:, SK * s:SK * s + SK, bass.ds(i * CW + col, CW)])
        for base, w in ((G_C, mlstm_up_v), (G_D, w_out_v)):
            with sp.Fori(0, NCH) as i:
                for s in range(4):
                    load_stage(base, i, 4, s, w[:, SK * s:SK * s + SK, bass.ds(i * CW, CW)])

        def expert_load(i, k, src):
            sp.wait_ge(lo_done, i * 48 + (G_END + k - RAW_M + 1))
            if k == 2:
                sp.wait_ge(sub_done, 4 * G_END)
            sp.dma_start(raw_m[k % RAW_M][:, :].rearrange("p (k n) -> p k n", k=SK),
                         src.rearrange("p e k n -> p (e k) n")).then_inc(raw_in_m[k % RAW_M], 16)

        sp.wait_ge(sub_done, 4 * G_D)
        with sp.Fori(0, EP) as i:
            for e in range(2):
                for n, w in enumerate((gate_v, up_v)):
                    for c in range(2):
                        for s in range(4):
                            expert_load(i, 16 * e + 8 * n + 4 * c + s,
                                        w[:, bass.ds(2 * i + e, 1), SK * s:SK * s + SK, c * CW:(c + 1) * CW])
            for c in range(NCH):
                for e in range(2):
                    for s in range(2):
                        expert_load(i, 32 + 4 * c + 2 * e + s,
                                    down_v[:, bass.ds(2 * i + e, 1), SK * s:SK * s + SK, c * CW:(c + 1) * CW])
        for t in range(TT):
            sp.wait_ge(o_rdy, t + 1)
            sp.dma_start(out_v[:, t, :], acc[:, t, :]).then_inc(out_st, 16)
        sp.wait_ge(out_st, 16 * TT)

    @block.gpsimd
    def _(pl):
        order = Order(pl, pool)
        taker = WaitTaker(pl)
        order.add(pl.memset(ident[:, :], 0.0))
        order.wait()
        pl.affine_select(out=ident[:, :], in_=ident[:, :], compare_op=ALU.not_equal, fill=1.0, base=0,
                         pattern=[[-1, P]], channel_multiplier=1).then_inc(id_rdy, 1)
        pl.dma_start(wif[:, :, :], w_in_v[:, :, COL_IF:COL_IF + NG]).then_inc(wif_in, 16)
        pl.dma_start(bias_if[0:NG, :], b_if.rearrange("o n -> n o"), allow_slow_non_contiguous=True)\
          .then_inc(par_in, 16)
        pl.dma_start(ps_col[:, :], pool_scale[0].rearrange("(k p) -> p k", p=P),
                     allow_slow_non_contiguous=True).then_inc(par_in, 16)
        pl.dma_start(nw_col[:, :], mlstm_norm_w[0].rearrange("(k p) -> p k", p=P),
                     allow_slow_non_contiguous=True).then_inc(par_in, 16)
        order.add(pl.memset(halves[:, :], 0.0))
        order.add(pl.memset(v_one[:, :], 1.0))
        order.add(pl.memset(behind[:, :, :], 0.0))
        order.wait()
        for d, sign in ((0, 1), (1, -1)):
            order.add(pl.affine_select(out=behind[:, d, :], in_=behind[:, d, :], compare_op=ALU.is_ge, fill=NEG,
                                       base=0, pattern=[[sign, P]], channel_multiplier=-sign))
        order.add(pl.affine_select(out=halves[:, :], in_=halves[:, :], compare_op=ALU.not_equal, fill=1.0, base=0,
                                   pattern=[[-1, CAP]], channel_multiplier=1))
        order.wait()
        pl.affine_select(out=halves[:, :], in_=halves[:, :], compare_op=ALU.not_equal, fill=1.0,
                         base=-CAP, pattern=[[-1, CAP]], channel_multiplier=1).then_inc(consts, 1)
        pl.iota(slot_no[:, :], pattern=[[0, 2], [1, CAP]], base=0, channel_multiplier=0,
                allow_small_or_imprecise_dtypes=True).then_inc(consts, 1)
        pl.iota(token_no[:, :], pattern=[[P, TT]], base=0, channel_multiplier=1,
                allow_small_or_imprecise_dtypes=True).then_inc(consts, 1)
        order.add(pl.memset(redge[:, :, :], 0.0))
        order.wait()
        for w, win in enumerate(WINDOWS):
            h = win // 2
            for t in range(PAD):
                order.add(pl.memset(redge[:, w, t:t + 1], 1.0 / (min(t, h) + h)))
            for t in range(S - PAD, S):
                c = PAD + t - (S - PAD)
                order.add(pl.memset(redge[:, w, c:c + 1], 1.0 / (min(S - t, h) + h)))
        order.wait()
        pl.memset(pool_u[:, :, 0:PAD], 0.0).then_inc(consts, 1)
        pl.memset(pool_u[:, :, PAD + S:], 0.0).then_inc(consts, 1)
        for n, s_ in enumerate(ahead):
            pl.memset(credit[:, n:n + 1], 0.0).then_inc(s_, 1)
        pl.wait_ge(xT_ps, KT)
        pl.dma_start(grp_raw[:, :, :], w_pool_grp[0].rearrange("(j g) (c p) n -> p j (g c) n", j=2, p=P))\
          .then_inc(grp_in, 16)
        pl.wait_ge(neg_rdy, 1)
        pl.dma_start(gate_rows_d.rearrange("d h s -> h d s"), g_neg[0:HEADS, :, :]).then_inc(neg_st, 16)

        def stored(st, i, free):
            col = ahead.index(free)
            pl.wait_ge(st, 16 * i + 16)
            pl.wait_ge(free, i + 1)
            pl.tensor_tensor(credit[:, col:col + 1], ident[:, 0:1], ident[:, 0:1], ALU.add).then_inc(free, 1)

        with pl.Fori(0, NCH) as i:
            pl.wait_ge(unit_out, 8 * i + (4 * U_A + 8))
            pl.dma_start(zp_v[:, bass.ds(4 * i, 4), :], zt[:, :, :]).then_inc(zp_st, 16)
            stored(zp_st, i, zt_free)
        pl.wait_ge(sub_done, 4 * G_B)
        pl.wait_ge(neg_st, 16)
        pl.wait_ge(zp_st, 16 * NCH)
        some = v_one[:, :].rearrange("p (t h n) -> p t h n", t=TT, h=2)
        pl.tensor_tensor(v_hi[:, :, :, HD:HD + 2], some, some, ALU.mult).then_inc(v_ones, 1)
        pl.tensor_tensor(v_lo[:, :, :, HD:HD + 2], some, some, ALU.subtract).then_inc(v_ones, 1)

        def decay_rows(i, h):
            src = gate_rows_d[:, bass.ds(2 * i + h, 1), :].rearrange("d h s -> h d s")
            pl.dma_start(gb[:, :, :], src.to_broadcast((P, 2, S))).then_inc(gb_in, 16)
            pl.wait_ge(gb_in, 32 * i + 16 * (h + 1))
            for d in range(2):
                pl.tensor_tensor(gd[:, d, :].rearrange("p (t n) -> p t n", t=TT),
                                 gb[:, d, :].rearrange("p (t n) -> p t n", t=TT),
                                 behind[:, d:d + 1, :].to_broadcast((P, TT, P)), ALU.add).then_inc(gd_rdy, 1)

        def store_heads(i):
            pl.wait_ge(hg_rdy, 4 * i + 4 + 1)
            pl.dma_start(hg_v[:, bass.ds(4 * i, 4), :], so[:, :, :]).then_inc(hg_st, 16)

        with pl.Fori(0, PAIRS - 1) as i:
            decay_rows(i, 0)
            pl.wait_ge(e_rdy, 28 * i + 14)
            decay_rows(i, 1)
            store_heads(i)
            pl.wait_ge(unit_out, 20 * i + (4 * U_B + 20))
            taker.take_wait()
            pl.dma_start(sgm_v[:, bass.ds(4 * i, 4), :], sgm[:, :, :]).then_inc(sgm_st, 16)
            stored(hg_st, i, so_free)
            stored(sgm_st, i, sgm_free)
        i = PAIRS - 1
        decay_rows(i, 0)
        pl.wait_ge(e_rdy, 28 * i + 14)
        decay_rows(i, 1)
        store_heads(i)
        for c in range(NCH - 1):
            pl.dma_start(hraw[:, c, :, :], hg_v[:, 4 * c:4 * c + 4, :]).then_inc(hraw_in[c], 16)
        pl.wait_ge(hg_st, 16 * PAIRS)
        pl.dma_start(hraw[:, i, :, :], hg_v[:, 4 * i:4 * i + 4, :]).then_inc(hraw_in[i], 16)
        pl.wait_ge(unit_out, 4 * (U_B + 5 * PAIRS))
        pl.dma_start(sgm_v[:, 4 * i:4 * i + 4, :], sgm[:, :, :]).then_inc(sgm_st, 16)
        pl.wait_ge(sgm_st, 16 * PAIRS)

        def load_cz(i, s):
            pl.dma_start(cz[:, s % 2, 0:1, :], sgm_v[:, bass.ds(4 * i + s, 1), :]).then_inc(cz_in[s % 2], 16)
            pl.dma_start(cz[:, s % 2, 1:2, :], zp_v[:, bass.ds(4 * i + s, 1), :]).then_inc(cz_in[s % 2], 16)

        load_cz(0, 0)
        load_cz(0, 1)
        with pl.Fori(0, NCH - 1) as i:
            for s in range(4):
                pl.wait_ge(z_lo, 4 * i + s + 1)
                load_cz(i, s + 2)
        for s in range(2):
            pl.wait_ge(z_lo, 4 * (NCH - 1) + s + 1)
            load_cz(NCH - 1, s + 2)
        pl.wait_ge(z_lo, KT)
        with pl.Fori(0, NCH) as i:
            pl.wait_ge(unit_out, 4 * i + 4 * U_D)
            pl.dma_start(xc[:, :, :], x_v[:, :, bass.ds(i * CW, CW)]).then_inc(xc_in, 16)
        pl.dma_start(lng1[:, :], ln1_g[0:1, :].to_broadcast((P, D))).then_inc(ln_in, 16)
        pl.dma_start(lnb1[:, :], ln1_b[0:1, :].to_broadcast((P, D))).then_inc(ln_in, 16)
        pl.wait_ge(sub_done, 4 * G_END)
        pl.dma_start(wr[:, :, :], tiles_of_rows(w_router[0])).then_inc(wr_in, 16)
        for t in range(TT):
            pl.wait_ge(x1_rdy, t + 1)
            pl.dma_start(x1_d[t * P:(t + 1) * P, :], acc[:, t, :]).then_inc(x1_st, 16)
        pl.wait_ge(x1_st, 16 * TT)

        def gather():
            pl.indirect_dma_start(xe[:, :], None, x1_d, bass.IndirectOffsetOnAxis(ap=tok_u[:, 0:1], axis=0))\
              .then_inc(xe_in, 16)

        pl.wait_ge(tok_rdy, 1)
        gather()
        with pl.Fori(1, EP) as i:
            pl.wait_ge(xeT_ps, 4 * i)
            pl.wait_ge(tok_rdy, i + 1)
            taker.take_wait()
            gather()
        count = pl.snap(taker.reg)
        pl.wait_ge(slots_free, 48 * (EP - 1) + 32 + HL_M)
        pl.wait_ge(lo_done, count)
        pl.dma_start(lng2[:, :], ln2_g[0:1, :].to_broadcast((P, D))).then_inc(ln2_in, 16)
        pl.dma_start(lnb2[:, :], ln2_b[0:1, :].to_broadcast((P, D))).then_inc(ln2_in, 16)

    @block.tensor
    def _(pe):
        mm = nc.tensor.matmul

        def transpose(o, src, n=P):
            return nc.tensor.transpose(o, src, ident[0:n, 0:n])

        pe.wait_ge(id_rdy, 1)
        for kt in range(KT):
            if kt % SK == 0:
                pe.wait_ge(x_in[kt // SK], 16)
            if kt >= 8:
                pe.wait_ge(xT_lo, kt - 7)
            for t in range(TT):
                c = kt % SK
                last = transpose(ps[:, kt % 8, t * P:(t + 1) * P], xst[:, kt // SK, t, c * P:(c + 1) * P])
            last.then_inc(xT_ps, 1)
        pe.wait_ge(xT_lo, KT)

        def gates():
            pe.wait_ge(wif_l, 1)
            o = X[0][0:NG, :]
            for kt in range(KT):
                mm(o, wif_hi[:, kt, :], xhi[:, kt, :], start=kt == 0, stop=False)
                mm(o, wif_hi[:, kt, :], xlo[:, kt, :], start=False, stop=False)
                last_ = mm(o, wif_lo[:, kt, :], xhi[:, kt, :], start=False, stop=kt == KT - 1)
            last_.then_inc(gate_ps, 1)

        def stage(base, i, per, k, s, n_stages, natural, mhi, mlo, unit):
            pe.wait_ge(lo_done, i * per + (base + k + 1))
            for sub_ in range(4):
                if s == 0 and (per or unit):
                    pe.wait_ge(unit_out, unit * 4 - 3 + sub_)
                cols = slice(sub_ * P, (sub_ + 1) * P)
                for r in range(SK):
                    kt = SK * s + r
                    first, stop = kt == 0, kt == SK * n_stages - 1
                    wh, wl = whi[k % HL][:, r, :], wlo[k % HL][:, r, :]
                    ah, al = mhi(kt), mlo(kt)
                    if natural:
                        mm(U[sub_], ah[:, cols], wh, start=first, stop=False)
                        mm(U[sub_], ah[:, cols], wl, start=False, stop=False)
                        last_ = mm(U[sub_], al[:, cols], wh, start=False, stop=stop)
                    else:
                        mm(U[sub_], wh[:, cols], ah, start=first, stop=False)
                        mm(U[sub_], wh[:, cols], al, start=False, stop=False)
                        last_ = mm(U[sub_], wl[:, cols], ah, start=False, stop=stop)
                last_.then_inc(sub_done, 1)

        def row_tile(a):
            return lambda kt: a[:, kt, :]

        X_IN = (row_tile(xhi), row_tile(xlo))
        PM_IN = (row_tile(pmhi), pmlo)

        def pool_groups(j):
            pe.wait_ge(dlo_rdy, 2 * j + 2)
            pe.wait_ge(grpl, j + 1)
            for gg in range(2):
                for es in range(2):
                    n = 2 * gg + es
                    for ct in range(2):
                        w = slice((gg * 2 + ct) * GD + es * P, (gg * 2 + ct) * GD + (es + 1) * P)
                        a = 2 * gg + ct
                        mm(X[n], grp_hi[:, w], dhi[:, a, :], start=ct == 0, stop=False)
                        mm(X[n], grp_hi[:, w], dlo[:, a, :], start=False, stop=False)
                        last_ = mm(X[n], grp_lo[:, w], dhi[:, a, :], start=False, stop=ct == 1)
                    last_.then_inc(grp_ps, 1)

        for s in range(4):
            stage(G_POOL, 0, 0, s, s, 4, False, *X_IN, 0)
            if s == 0:
                gates()
        pe.wait_ge(gate_rdy, 1)
        for k in range(4):
            last = mm(X[k][0:HEADS, :], ident[0:NG, HEADS * k:HEADS * (k + 1)], gate_log if k % 2 else gate_pre,
                      start=True, stop=True)
        last.then_inc(rows_ps, 1)
        for s in range(4):
            if s == 2:
                pe.wait_ge(em_rdy, 1)
                for kind, src in ((0, g_a), (1, g_em)):
                    for d in range(2):
                        for t in range(TT):
                            n = ((kind * 2 + d) * TT + t) * HEADS
                            last = transpose(X[0][:, n:n + HEADS], src[0:HEADS, d, t * P:(t + 1) * P], HEADS)
                last.then_inc(col_ps, 1)
            if s == 3:
                pe.wait_ge(col_rdy, 2)
                pool_groups(0)
            stage(G_POOL, 0, 0, 4 + s, s, 4, False, *X_IN, 1)

        def two_chunks(i, first):
            for j in range(2):
                for s in range(4):
                    if first and j == 0 and s == 2:
                        pe.wait_ge(pm_lo, 4)
                        pool_groups(1)
                    stage(G_A, i, 12, 6 * j + s, s, 4, False, *X_IN, 4 * i + (U_A + 2 * j))
                if first and j == 0:
                    pe.wait_ge(pm_lo, PW // P)
                for s in range(2):
                    stage(G_A, i, 12, 6 * j + 4 + s, s, 2, False, *PM_IN, 4 * i + (U_A + 2 * j + 1))

        two_chunks(0, True)
        with pe.Fori(1, NCH // 2) as i:
            two_chunks(i, False)

        def scores(h):
            for kt in range(TT):
                for c in range(2):
                    n, keys = 2 * h + c, slice(kt * P, (kt + 1) * P)
                    mm(X[kt], k_hi[:, n, keys], q_hi[:, n, :], start=c == 0, stop=False)
                    mm(X[kt], k_hi[:, n, keys], q_lo[:, n, :], start=False, stop=False)
                    last_ = mm(X[kt], k_lo[:, n, keys], q_hi[:, n, :], start=False, stop=c == 1)
                last_.then_inc(s_ps, 1)

        def values(h, d):
            for qt in range(TT):
                keys = range(qt + 1) if d == 0 else range(qt, TT)
                for kt in keys:
                    at = (F_OFF[kt] + (qt - kt) * P) if d == 0 else (B_OFF[kt] + qt * P)
                    o, a = X[qt][:, 0:HD + 2], a_hi[:, d, at:at + P]
                    mm(o, a, v_hi[:, kt, h, :], start=kt == keys[0], stop=False)
                    mm(o, a, v_lo[:, kt, h, :], start=False, stop=False)
                    last_ = mm(o, a_lo[:, d, at:at + P], v_hi[:, kt, h, :], start=False,
                               stop=kt == keys[-1])
                last_.then_inc(av_ps, 1)

        def head_back(h):
            for c in range(2):
                for t in range(TT):
                    last_ = transpose(X[c][:, t * P:(t + 1) * P], hh[h][:, t, c * P:(c + 1) * P])
                last_.then_inc(ht_ps, 1)

        with pe.Fori(0, PAIRS) as i:
            for k in range(20):
                if k == 9:
                    pe.wait_ge(unit_out, 20 * i + 4 * (U_B + 2))
                    pe.wait_ge(hg_rdy, 4 * i + 1)
                    scores(0)
                if k == 12:
                    pe.wait_ge(a_rdy, 16 * i + 8)
                    scores(1)
                if k == 13:
                    pe.wait_ge(a_rdy, 16 * i + 16)
                    pe.wait_ge(unit_out, 20 * i + 4 * (U_B + 3))
                    pe.wait_ge(v_ones, 2)
                    pe.wait_ge(a_lo_rdy, 4 * i + 2)
                    values(0, 0)
                if k == 14:
                    pe.wait_ge(hf_rdy, 8 * i + 4)
                    values(0, 1)
                if k == 15:
                    pe.wait_ge(hn_rdy, 8 * i + 4)
                    pe.wait_ge(a_lo_rdy, 4 * i + 4)
                    values(1, 0)
                if k == 16:
                    pe.wait_ge(hf_rdy, 8 * i + 8)
                    values(1, 1)
                if k == 17:
                    pe.wait_ge(hn_rdy, 8 * i + 8)
                    head_back(0)
                if k == 18:
                    pe.wait_ge(hg_rdy, 4 * i + 2 + 1)
                    head_back(1)
                stage(G_B, i, 20, k, k % 4, 4, k // 4 == 2, *X_IN, 5 * i + (U_B + k // 4))
        with pe.Fori(0, NCH) as i:
            for s in range(4):
                pe.wait_ge(hgs_lo, s + 1)
                stage(G_C, i, 4, s, s, 4, False, row_tile(hghi), row_tile(hglo), i + U_C)
        with pe.Fori(0, NCH) as i:
            for s in range(4):
                pe.wait_ge(z_lo, SK * (s + 1))
                stage(G_D, i, 4, s, s, 4, True, row_tile(zhi), row_tile(zlo), i + U_D)

        pe.wait_ge(consts, 5)
        pe.wait_ge(unit_out, 4 * (U_D + NCH))
        pe.wait_ge(wr_in, 16)

        def x1_across(t):
            pe.wait_ge(x1_rdy, t + 1)
            if t >= 2:
                pe.wait_ge(lgT_rdy, t - 1)
            for b in range(4):
                for r in range(4):
                    kt = 4 * b + r
                    last_ = transpose(ps[:, 4 * (t % 2) + b, r * P:(r + 1) * P], acc[:, t, kt * P:(kt + 1) * P])
                last_.then_inc(x1T_ps, 1)

        def logits(t):
            pe.wait_ge(x1T_rdy, 4 * t + 4)
            for kt in range(KT):
                last_ = mm(ps[0:NE, 4 * (t % 2), 0:P], wr[:, kt, :], x1T[t % 2][:, kt, :], start=kt == 0,
                           stop=kt == KT - 1)
            last_.then_inc(lg_ps, 1)

        x1_across(0)
        for t in range(1, TT):
            x1_across(t)
            logits(t - 1)
        logits(TT - 1)
        pe.wait_ge(lgT_rdy, TT)
        for t in range(TT):
            last = transpose(X[1][:, t * NE:(t + 1) * NE], lgT[0:NE, t * P:(t + 1) * P], NE)
        last.then_inc(lg_ps, 1)
        pe.wait_ge(aff_rdy, 1)
        for t in range(TT):
            last = transpose(X[2][0:NE, t * P:(t + 1) * P], aff_c[:, t, :])
        last.then_inc(affT_ps, 1)
        pe.wait_ge(slot_rdy, 1)
        for t in range(TT):
            last = transpose(X[0][:, t * NE:(t + 1) * NE], slot_r[0:NE, t * P:(t + 1) * P], NE)
            if t < TT - 1:
                last.then_inc(slots_free, 1)
        last.then_inc(slotT_ps, 1)

        def tokens_of_slots(q):
            pe.wait_ge(oh_rdy, 8 * q + 8)
            for e in range(2):
                for t in range(TT):
                    last_ = mm(X[2][e * CAP:(e + 1) * CAP, 0:1], onehot[:, e, t, 0:CAP], token_no[:, t:t + 1],
                               start=t == 0, stop=t == TT - 1)
            last_.then_inc(tok_ps, 1)

        def gathered_back(q):
            pe.wait_ge(xe_in, 16 * q + 16)
            for b in range(4):
                for r in range(4):
                    kt = 4 * b + r
                    last_ = transpose(X[b][:, r * P:(r + 1) * P], xe[:, kt * P:(kt + 1) * P])
                last_.then_inc(xeT_ps, 1)

        tokens_of_slots(0)
        pe.wait_ge(tok_rdy, 1)
        gathered_back(0)
        pe.wait_ge(xeT_lo, 4)

        def scatter_and_weights(q):
            for e in range(2):
                for t in range(TT):
                    last_ = transpose(X[e][:, t * P:(t + 1) * P], onehot[:, e, t, :])
                last_.then_inc(scat_ps, 1)
            for e in range(2):
                for t in range(TT):
                    last_ = mm(X[3][:, e:e + 1], onehot[:, e, t, :], aff_c[:, t, bass.ds(2 * q + e, 1)],
                               start=t == 0, stop=t == TT - 1)
            last_.then_inc(gw_ps, 1)

        def halves_added():
            for n in range(2):
                for f in range(FT):
                    last_ = mm(X[n][:, f * CAP:(f + 1) * CAP], gu[:, n, f * P:(f + 1) * P], halves[:, :],
                               start=True, stop=True)
                last_.then_inc(guT_ps, 1)

        def combine(c):
            for t in range(TT):
                for e in range(2):
                    w = scat[:, e, t * P:(t + 1) * P]
                    mm(X[t], w, yhi[c % 2][:, e, :], start=e == 0, stop=False)
                    last_ = mm(X[t], w, ylo[c % 2][:, e, :], start=False, stop=e == 1)
                last_.then_inc(comb_ps, 1)

        def steps(q, first, end, last_pair=False):
            for k in range(first, end):
                if k == 2:
                    pe.wait_ge(acc_add, 4 * q + 1)
                    scatter_and_weights(q)
                if k == 17:
                    pe.wait_ge(scat_rdy, 2 * q + 2)
                    pe.wait_ge(gu_rdy, 8 * q + 4)
                    halves_added()
                if k == 20 and not last_pair:
                    tokens_of_slots(q + 1)
                if k == 33:
                    pe.wait_ge(hid_pre, 2 * q + 1)
                    pe.wait_ge(gu_rdy, 8 * q + 8)
                    halves_added()
                if k == 34 and not last_pair:
                    pe.wait_ge(tok_rdy, q + 2)
                    pe.wait_ge(hid_pre, 2 * q + 2)
                    pe.wait_ge(gw_rdy, q + 1)
                    gathered_back(q + 1)
                if k in (38, 42, 46):
                    c = (k - 38) // 4
                    pe.wait_ge(y_lo, 8 * q + 2 * c + 2 + 1)
                    if c == 0 and last_pair:
                        pe.wait_ge(hid_pre, 2 * q + 2)
                        pe.wait_ge(gw_rdy, q + 1)
                    elif c == 0:
                        pe.wait_ge(xeT_lo, 4 * q + 8)
                    else:
                        pe.wait_ge(acc_add, 4 * q + c + 1)
                    combine(c)
                pe.wait_ge(lo_done, 48 * q + (G_END + k + 1))
                wh, wl = whi_m[k % HL_M], wlo_m[k % HL_M]
                if k < 32:
                    e, c, s, depth = k // 16, k % 16 // 4, k % 4, KT
                    bank = U[c]
                    if k == 0:
                        pe.wait_ge(xeT_lo, 4 * q + 4)
                    if k == 4:
                        pe.wait_ge(y_lo, 8 * q + 1)
                    if k >= 16 and s == 0:
                        pe.wait_ge(gu_rdy, 8 * q + 1 + c)
                    acts = [xeT[:, SK * s + r, e, :] for r in range(SK)]
                else:
                    c, e, s, depth = (k - 32) // 4, (k - 32) % 4 // 2, k % 2, FT
                    bank = U[2 * e + c % 2]
                    if s == 0 and c == 0:
                        pe.wait_ge(hid_lo, 2 * q + e + 1 + 1)
                        pe.wait_ge(gu_rdy, 8 * q + 5)
                    if s == 0 and c >= 2:
                        pe.wait_ge(y_lo, 8 * q + 2 * (c - 2) + e + 1 + 1)
                    acts = [hid[e][:, SK * s + r, :] for r in range(SK)]
                for r in range(SK):
                    n = SK * s + r
                    mm(bank, acts[r], wh[:, r, :], start=n == 0, stop=False)
                    last_ = mm(bank, acts[r], wl[:, r, :], start=False, stop=n == depth - 1)
                last_.then_inc(slots_free, 1)

        def last_columns(q):
            pe.wait_ge(y_lo, 8 * q + 8 + 1)
            pe.wait_ge(acc_add, 4 * q + 3 + 1)
            combine(3)

        steps(0, 0, 2)
        with pe.Fori(0, EP - 1) as i:
            steps(i, 2, 48)
            steps(i + 1, 0, 1)
            last_columns(i)
            steps(i + 1, 1, 2)
        steps(EP - 1, 2, 48, True)
        last_columns(EP - 1)

    @block.scalar
    def _(sc):
        A = nc.scalar.activation
        order = Order(sc, act)

        def split(base, i, per, k):
            n = base + k
            sc.wait_ge(raw_in[k % RAW], i * (16 * (per // RAW)) + 16 * (n // RAW + 1))
            if n >= HL:
                sc.wait_ge(sub_done, i * (4 * per) + 4 * (n - HL + 1))
            A(whi[k % HL][:, :, :].rearrange("p k n -> p (k n)"), raw[k % RAW][:, :], ACT.Copy).then_inc(hi_done, 1)

        def read_out(base, i, per, k, dst, func):
            for sub_ in range(4):
                sc.wait_ge(sub_done, i * (4 * per) + (4 * (base + k) + sub_ + 1))
                A(dst(sub_), U[sub_], func).then_inc(unit_out, 1)

        for kt in range(KT):
            sc.wait_ge(xT_ps, kt + 1)
            A(xhi[:, kt, :], ps[:, kt % 8, :], ACT.Copy).then_inc(xT_hi, 1)
        split(G_POOL, 0, 0, 0)
        sc.wait_ge(wif_in, 16)
        A(wif_hi[:, :, :], wif[:, :, :], ACT.Copy).then_inc(wif_h, 1)

        def log_sigmoids():
            sc.wait_ge(gate_ps, 1)
            sc.wait_ge(par_in, 48)
            A(gate_pre, X[0][0:NG, :], ACT.Identity, bias=bias_if[0:NG, 0:1]).then_inc(pre_rdy, 1)
            sc.wait_ge(pre_rdy, 1)
            order.add(A(gate_log, gate_pre, ACT.Abs))
            order.wait()
            order.add(A(gate_log, gate_log, ACT.Exp, scale=-1.0))
            order.wait()
            A(gate_log, gate_log, ACT.Ln, bias=1.0).then_inc(soft_rdy, 1)

        def group_weights(j):
            sc.wait_ge(grp_in, 16)
            if j:
                sc.wait_ge(grp_ps, 4)
            A(grp_hi[:, :], grp_raw[:, j, :], ACT.Copy).then_inc(grph, 1)

        def differences(j, gg):
            sc.wait_ge(diff_rdy, 2 * j + gg + 1)
            if j:
                sc.wait_ge(grp_ps, 4)
            src = (sum_a if gg == 0 else sum_b)[:, :, PAD:PAD + S]
            A(dhi[:, 2 * gg:2 * gg + 2, :], src, ACT.Copy).then_inc(dhi_rdy, 1)

        def groups_out(j):
            for n in range(4):
                sc.wait_ge(grp_ps, 4 * j + n + 1)
                A(pmhi[:, 4 * j + n, :], X[n], ACT.Copy, scale=ps_col[:, 4 * j + n:4 * j + n + 1]).then_inc(pm_hi, 1)

        for k in range(8):
            split(G_POOL, 0, 0, k + 1)
            if k == 1:
                log_sigmoids()
            if k == 3:
                read_out(G_POOL, 0, 0, k, lambda n: pool_u[:, n, PAD:PAD + S], ACT.Copy)
            if k == 4:
                sc.wait_ge(m_rdy, 1)
                A(g_em[0:HEADS, :, :], g_m[0:HEADS, :, :], ACT.Exp, scale=-1.0).then_inc(em_rdy, 1)
                group_weights(0)
            if k == 5:
                differences(0, 0)
                differences(0, 1)
            if k == 7:
                sc.wait_ge(neg_st, 16)
                groups_out(0)
                group_weights(1)
                sc.wait_ge(dlo_rdy, 2)
                read_out(G_POOL, 0, 0, k, lambda n: pool_u[:, n, PAD:PAD + S], ACT.Copy)

        def two_chunks(i, first):
            for k in range(12):
                split(G_A, i, 12, k + 1)
                if first and k < 2:
                    differences(1, k)
                if first and k == 2:
                    groups_out(1)
                if k % 6 == 3:
                    read_out(G_A, i, 12, k, lambda n: sgp[:, n, :], ACT.Sigmoid)

        two_chunks(0, True)
        with sc.Fori(1, NCH // 2) as i:
            two_chunks(i, False)

        def hi_out(i, k, hi):
            for n in range(4):
                sc.wait_ge(sub_done, 80 * i + (4 * (G_B + k) + n + 1))
                A(hi(n), U[n], ACT.Copy).then_inc(kqv_hi, 1)

        def scores_hi(i, h):
            for d in range(2):
                sc.wait_ge(a_rdy, 16 * i + 8 * h + 8)
                A(a_hi[:, d, :], amat[:, d, :], ACT.Copy).then_inc(a_hi_rdy, 1)

        def decays(i, h):
            sc.wait_ge(gd_rdy, 4 * i + 2 * h + 2)
            for kt in range(TT):
                for d in range(2):
                    bias = a_col[:, bass.ds(2 * i + h, 1), d, kt:kt + 1].rearrange("p a b -> p (a b)")
                    own = slice(kt * P, (kt + 1) * P)
                    off = F_OFF[kt] if d == 0 else B_OFF[kt]
                    here = off if d == 0 else off + kt * P
                    A(amat[:, d, here:here + P], gd[:, d, own], ACT.Exp, bias=bias).then_inc(e_rdy, 1)
                    rest = slice((kt + 1) * P, S) if d == 0 else slice(0, kt * P)
                    n = rest.stop - rest.start
                    if n:
                        there = off + P if d == 0 else off
                        A(amat[:, d, there:there + n], gb[:, d, rest], ACT.Exp, bias=bias).then_inc(e_rdy, 1)

        def denominator(i, h, d):
            sc.wait_ge(av_ps, 16 * i + 8 * h + 4 * d + 4)
            A(den[:, d, :], Xall[:, :, HD], ACT.Abs).then_inc(den_abs, 1)

        def forward_out(i, h):
            sc.wait_ge(rec_rdy, 4 * i + 2 * h + 1)
            for t in range(TT):
                A(hh[h][:, t, :], X[t][:, 0:HD], ACT.Copy, scale=den[:, 0, t:t + 1]).then_inc(hf_rdy, 1)

        def head_root(i, h):
            sc.wait_ge(var_rdy, 2 * i + h + 1)
            A(rstd[:, :], mv[:, :, 1], ACT.Sqrt, bias=geps[:, 0:1]).then_inc(sq_rdy, 1)

        with sc.Fori(0, PAIRS) as i:
            for k in range(20):
                split(G_B, i, 20, k + 1)
                if k == 3:
                    sc.wait_ge(v_ones, 2)
                    sc.wait_ge(sgm_free, i + 1)
                    hi_out(i, k, lambda n: k_hi[:, n, :])
                if k == 7:
                    sc.wait_ge(so_free, i + 1)
                    hi_out(i, k, lambda n: q_hi[:, n, :])
                if k == 8:
                    decays(i, 0)
                if k == 10:
                    scores_hi(i, 0)
                if k == 11:
                    sc.wait_ge(a_lo_rdy, 4 * i + 2)
                    decays(i, 1)
                    hi_out(i, k, lambda n: v_hi[:, n, :, 0:HD])
                if k == 13:
                    denominator(i, 0, 0)
                    forward_out(i, 0)
                if k == 14:
                    denominator(i, 0, 1)
                    scores_hi(i, 1)
                    head_root(i, 0)
                if k == 15:
                    denominator(i, 1, 0)
                    forward_out(i, 1)
                    read_out(G_B, i, 20, k, lambda n: so[:, n, :], ACT.Sigmoid)
                if k == 16:
                    denominator(i, 1, 1)
                    head_root(i, 1)
                if k == 19:
                    read_out(G_B, i, 20, k, lambda n: sgm[:, n, :], ACT.Sigmoid)
        for c in range(NCH):
            sc.wait_ge(hraw_in[c], 16)
            A(hghi[:, 4 * c:4 * c + 4, :], hraw[:, c, :, :], ACT.Copy).then_inc(hgs_hi, 1)

        def z_parts(i):
            for n in range(4):
                sc.wait_ge(z_rdy, 4 * i + n + 1)
                A(zhi[:, bass.ds(4 * i + n, 1), :], cz[:, n % 2, 1:2, :], ACT.Copy).then_inc(z_hi, 1)

        with sc.Fori(0, NCH) as i:
            for k in range(4):
                split(G_C, i, 4, k + 1)
                if k == 3:
                    z_parts(i)
        with sc.Fori(0, NCH - 1) as i:
            for k in range(4):
                split(G_D, i, 4, k + 1)
        for k in range(3):
            split(G_D + 4 * (NCH - 1), 0, 0, k + 1)

        sc.wait_ge(var1_rdy, 1)
        A(rstd[:, :], mv[:, :, 1], ACT.Sqrt, bias=leps[:, 0:1]).then_inc(sq1_rdy, 1)
        def logits_out(t):
            sc.wait_ge(lg_ps, t + 1)
            A(lgT[0:NE, t * P:(t + 1) * P], ps[0:NE, 4 * (t % 2), 0:P], ACT.Copy).then_inc(lgT_rdy, 1)

        for t in range(TT):
            for b in range(4):
                sc.wait_ge(x1T_ps, 4 * t + b + 1)
                A(x1T[t % 2][:, 4 * b:4 * b + 4, :], ps[:, 4 * (t % 2) + b, :], ACT.Copy).then_inc(x1T_rdy, 1)
            if t:
                logits_out(t - 1)
        logits_out(TT - 1)
        sc.wait_ge(lg_max, 1)
        A(sm_exp[:, :, :], sm_exp[:, :, :], ACT.Exp).then_inc(lg_exp, 1)
        sc.wait_ge(x1_st, 16 * TT)
        for t in range(TT):
            A(acc[:, t, :], acc[:, t, :], ACT.Copy, scale=ALPHA).then_inc(acc_scaled, 1)

        def split_m(q, k):
            sc.wait_ge(raw_in_m[k % RAW_M], q * (16 * 48 // RAW_M) + 16 * (k // RAW_M + 1))
            sc.wait_ge(slots_free, 48 * q + (k + 1))
            A(whi_m[k % HL_M][:, :, :].rearrange("p k n -> p (k n)"), raw_m[k % RAW_M][:, :], ACT.Copy)\
                .then_inc(hi_done, 1)

        def tokens_hi(q):
            for b in range(4):
                sc.wait_ge(xeT_ps, 4 * q + b + 1)
                A(xeT[:, 4 * b:4 * b + 4, :, 0:CAP], X[b].rearrange("p (r e n) -> p r e n", r=4, e=2), ACT.Copy)\
                    .then_inc(xeT_hi, 1)

        def hidden(q, e):
            sc.wait_ge(guT_ps, 4 * q + 2 * e + 1)
            sc.wait_ge(hid_lo, 2 * q + e + 1)
            A(hid_tmp[:, :], X[0], ACT.Sigmoid).then_inc(sig_rdy, 1)
            sc.wait_ge(hid_pre, 2 * q + e + 1)
            A(hid[e][:, :, 0:CAP], hid_tmp[:, :].rearrange("p (f n) -> p f n", f=FT), ACT.Copy).then_inc(hid_hi, 1)

        def steps(q, first, end, last_pair=False):
            for k in range(first, end):
                if k + AHEAD_M < 48:
                    split_m(q, k + AHEAD_M)
                elif not last_pair:
                    split_m(q + 1, k + AHEAD_M - 48)
                if k == 2:
                    for e in range(2):
                        sc.wait_ge(scat_ps, 2 * q + e + 1)
                        A(scat[:, e, :], X[e], ACT.Copy).then_inc(scat_rdy, 1)
                if k < 32 and k % 4 == 3:
                    c = k % 16 // 4
                    sc.wait_ge(slots_free, 48 * q + (k + 1 + HL_M))
                    A(gu[:, c // 2, c % 2 * CW:(c % 2 + 1) * CW], U[c], ACT.Copy).then_inc(gu_rdy, 1)
                if k == 17:
                    hidden(q, 0)
                if k == 33:
                    hidden(q, 1)
                if k >= 32 and k % 2 == 1:
                    c, e = (k - 32) // 4, (k - 32) % 4 // 2
                    sc.wait_ge(slots_free, 48 * q + (k + 1 + HL_M))
                    sc.wait_ge(gw_rdy, q + 1)
                    if c >= 2:
                        sc.wait_ge(comb_ps, 16 * q + 4 * (c - 1) + 1)
                    A(yhi[c % 2][:, e, :], U[2 * e + c % 2], ACT.Copy, scale=gate_w[:, e:e + 1]).then_inc(y_hi, 1)
                if k == 34 and not last_pair:
                    tokens_hi(q + 1)

        for k in range(AHEAD_M):
            split_m(0, k)
        tokens_hi(0)
        steps(0, 0, 2)
        with sc.Fori(0, EP - 1) as i:
            steps(i, 2, 48)
            steps(i + 1, 0, 2)
        steps(EP - 1, 2, 48, True)
        sc.wait_ge(o_var, 1)
        A(rstd[:, :], mv[:, :, 1], ACT.Sqrt, bias=leps[:, 0:1]).then_inc(o_sq, 1)

    @block.vector
    def _(ve):
        V = nc.vector
        order = Order(ve, dve)

        def less(o, a, hi):
            return V.tensor_tensor(o, a, hi.bitcast(F32), ALU.subtract)

        def split(base, i, per, k):
            ve.wait_ge(hi_done, i * per + (base + k + 1))
            less(wlo[k % HL][:, :, :].rearrange("p k n -> p (k n)"), raw[k % RAW][:, :],
                 whi[k % HL][:, :, :].rearrange("p k n -> p (k n)")).then_inc(lo_done, 1)

        order.add(V.memset(geps[:, :], GN_EPS))
        order.add(V.memset(leps[:, :], LN_EPS))
        for kt in range(KT):
            ve.wait_ge(xT_hi, kt + 1)
            less(xlo[:, kt, :], ps[:, kt % 8, :], xhi[:, kt, :]).then_inc(xT_lo, 1)
        split(G_POOL, 0, 0, 0)
        ve.wait_ge(wif_h, 1)
        less(wif_lo[:, :, :], wif[:, :, :], wif_hi[:, :, :]).then_inc(wif_l, 1)

        def log_sigmoids():
            ve.wait_ge(soft_rdy, 1)
            V.scalar_tensor_tensor(gate_log, gate_pre, 0.0, gate_log, ALU.min, ALU.subtract).then_inc(gate_rdy, 1)
            order.add(V.memset(g_ones[0:HEADS, :], 1.0))

        def scans():
            fwd, bwd = slice(None), slice(None, None, -1)
            ve.wait_ge(rows_ps, 1)
            order.wait()
            for d, way in ((0, fwd), (1, bwd)):
                order.add(V.tensor_tensor_scan(g_f[0:HEADS, d, way], g_ones[0:HEADS, :], X[2 * d + 1][0:HEADS, way],
                                               0.0, ALU.mult, ALU.add))
            order.wait()
            for d in range(2):
                order.add(V.tensor_tensor(g_a[0:HEADS, d, :], X[2 * d][0:HEADS, :], g_f[0:HEADS, d, :],
                                          ALU.subtract))
            order.wait()
            for d, way in ((0, fwd), (1, bwd)):
                order.add(V.tensor_tensor_scan(g_m[0:HEADS, d, way], g_a[0:HEADS, d, way], g_a[0:HEADS, d, way],
                                               0.0, ALU.max, ALU.max))
            order.wait()
            V.tensor_scalar(g_neg[0:HEADS, :, :], g_m[0:HEADS, :, :], -1.0, None, ALU.mult).then_inc(neg_rdy, 1)
            ve.wait_ge(neg_rdy, 1)
            V.tensor_tensor(g_m[0:HEADS, :, :], g_m[0:HEADS, :, :], g_f[0:HEADS, :, :], ALU.add).then_inc(m_rdy, 1)

        def columns():
            ve.wait_ge(col_ps, 1)
            cols = X[0][:, 0:4 * TT * HEADS].rearrange("p (k d t h) -> p k h d t", k=2, d=2, t=TT)
            V.tensor_copy(a_col[:, :, :, :], cols[:, 0]).then_inc(col_rdy, 1)
            V.tensor_copy(em_col[:, :, :, :], cols[:, 1]).then_inc(col_rdy, 1)

        def group_weights(j):
            ve.wait_ge(grph, j + 1)
            less(grp_lo[:, :], grp_raw[:, j, :], grp_hi[:, :]).then_inc(grpl, 1)

        def differences(j, gg):
            ve.wait_ge(unit_out, 4 * j + 4)
            ve.wait_ge(consts, 5)
            w, win = 2 * j + gg, WINDOWS[2 * j + gg]
            u = pool_u[:, 2 * gg:2 * gg + 2, :]
            src, bufs, lo, hi, step = u, [sum_a, sum_b], 1, S + 2 * PAD, 1
            order.wait()
            order.add(V.tensor_tensor(sum_a[:, :, 1:hi], u[:, :, 0:hi - 1], u[:, :, 1:hi], ALU.add))
            src, width, n = sum_a, 2, 1
            while width < win:
                step = width // 2
                lo, hi = lo + step, hi - step
                dst = bufs[n % 2]
                order.wait()
                order.add(V.tensor_tensor(dst[:, :, lo:hi], src[:, :, lo - step:hi - step],
                                          src[:, :, lo + step:hi + step], ALU.add))
                src, width, n = dst, 2 * width, n + 1
            order.wait()
            h = win // 2
            if h > 0:
                for edge, at in ((0, PAD), (PAD, S)):
                    sl = src[:, :, at:at + PAD]
                    order.add(V.scalar_tensor_tensor(
                        sl, sl, float(win), redge[:, w:w + 1, edge:edge + PAD].to_broadcast((P, 2, PAD)),
                        ALU.mult, ALU.mult))
            order.wait()
            V.scalar_tensor_tensor(src[:, :, PAD:PAD + S], src[:, :, PAD:PAD + S], 1.0 / win,
                                   u[:, :, PAD:PAD + S], ALU.mult, ALU.subtract).then_inc(diff_rdy, 1)
            ve.wait_ge(dhi_rdy, w + 1)
            less(dlo[:, 2 * gg:2 * gg + 2, :], src[:, :, PAD:PAD + S], dhi[:, 2 * gg:2 * gg + 2, :])\
                .then_inc(dlo_rdy, 1)
            ve.wait_ge(dlo_rdy, w + 1)

        def groups_out(j):
            for n in range(4):
                k = 4 * j + n
                ve.wait_ge(pm_hi, k + 1)
                V.scalar_tensor_tensor(pmlo(k), X[n], ps_col[:, k:k + 1], pmhi[:, k, :].bitcast(F32), ALU.mult,
                                       ALU.subtract).then_inc(pm_lo, 1)

        for k in range(8):
            split(G_POOL, 0, 0, k + 1)
            if k == 1:
                log_sigmoids()
            if k == 4:
                scans()
                group_weights(0)
            if k == 5:
                differences(0, 0)
                differences(0, 1)
            if k == 6:
                columns()
            if k == 7:
                groups_out(0)
                group_weights(1)

        def two_chunks(i, first):
            for k in range(12):
                split(G_A, i, 12, k + 1)
                if first and k < 2:
                    differences(1, k)
                if first and k == 2:
                    groups_out(1)
                if k % 6 == 5:
                    j = k // 6
                    ve.wait_ge(zt_free, 2 * i + j + 1)
                    for n in range(4):
                        ve.wait_ge(sub_done, 48 * i + (4 * (G_A + k) + n + 1))
                        if n == 0:
                            ve.wait_ge(unit_out, 16 * i + 4 * (U_A + 2 * j + 1))
                        V.tensor_tensor(zt[:, n, :], U[n], sgp[:, n, :], ALU.mult).then_inc(unit_out, 1)

        two_chunks(0, True)
        with ve.Fori(1, NCH // 2) as i:
            two_chunks(i, False)

        def lo_out(i, k, hi, lo):
            for n in range(4):
                ve.wait_ge(kqv_hi, 12 * i + (k - 3 + n + 1))
                less(lo(n), U[n], hi(n)).then_inc(unit_out, 1)

        def scores_lo(i, h):
            for d in range(2):
                ve.wait_ge(a_hi_rdy, 4 * i + 2 * h + d + 1)
                less(a_lo[:, d, :], amat[:, d, :], a_hi[:, d, :]).then_inc(a_lo_rdy, 1)

        def decayed_scores(i, h):
            ve.wait_ge(e_rdy, 28 * i + 14 * h + 14)
            for kt in range(TT):
                ve.wait_ge(s_ps, 8 * i + 4 * h + kt + 1)
                for d, off, (at, n) in ((0, F_OFF[kt], f_range(kt)), (1, B_OFF[kt], b_range(kt))):
                    a = amat[:, d, off:off + n]
                    V.scalar_tensor_tensor(a, X[kt][:, at:at + n], HD ** -0.5, a, ALU.mult, ALU.mult)\
                        .then_inc(a_rdy, 1)

        def reciprocals(i, h, d):
            em = em_col[:, bass.ds(2 * i + h, 1), d, :].rearrange("p a t -> p (a t)")
            ve.wait_ge(den_abs, 4 * i + 2 * h + d + 1)
            order.add(V.tensor_tensor(den[:, d, :], den[:, d, :], em, ALU.max))
            order.wait()
            V.reciprocal(den[:, d, :], den[:, d, :]).then_inc(rec_rdy, 1)

        def backward_and_norm(i, h):
            reciprocals(i, h, 1)
            ve.wait_ge(rec_rdy, 4 * i + 2 * h + 2)
            ve.wait_ge(hf_rdy, 8 * i + 4 * h + 4)
            for t in range(TT):
                o = hh[h][:, t, :]
                order.add(V.scalar_tensor_tensor(o, X[t][:, 0:HD], den[:, 1, t:t + 1], o, ALU.mult, ALU.add))
            order.wait()
            for t in range(TT):
                order.add(V.bn_stats(stat[:, t, 0, :], hh[h][:, t, :]))
            order.wait()
            order.add(V.memset(carrier[:, :], 0.0))
            for t in range(TT):
                last_ = V.bn_aggr(mv[:, t, :], stat[:, t, 0, :])
                if t < TT - 1:
                    order.add(last_)
            last_.then_inc(var_rdy, 1)
            order.wait()
            ve.wait_ge(sq_rdy, 2 * i + h + 1)
            order.add(V.reciprocal(rstd[:, :], rstd[:, :]))
            order.wait()
            for t in range(TT):
                V.tensor_scalar(hh[h][:, t, :], hh[h][:, t, :], mv[:, t, 0:1], rstd[:, t:t + 1], ALU.subtract,
                                ALU.mult).then_inc(hn_rdy, 1)

        def gated_head(i, h):
            for c in range(2):
                n = 2 * h + c
                ve.wait_ge(ht_ps, 4 * i + n + 1)
                nw = nw_col[:, bass.ds(4 * i + n, 1)]
                V.scalar_tensor_tensor(so[:, n, :], X[c], nw, so[:, n, :], ALU.mult, ALU.mult).then_inc(hg_rdy, 1)

        with ve.Fori(0, PAIRS) as i:
            order.loop(i, 30)
            for k in range(20):
                split(G_B, i, 20, k + 1)
                if k == 3:
                    lo_out(i, k, lambda n: k_hi[:, n, :], lambda n: k_lo[:, n, :])
                if k == 7:
                    lo_out(i, k, lambda n: q_hi[:, n, :], lambda n: q_lo[:, n, :])
                if k == 9:
                    decayed_scores(i, 0)
                if k == 10:
                    scores_lo(i, 0)
                if k == 12:
                    decayed_scores(i, 1)
                if k == 11:
                    lo_out(i, k, lambda n: v_hi[:, n, :, 0:HD], lambda n: v_lo[:, n, :, 0:HD])
                if k == 13:
                    reciprocals(i, 0, 0)
                if k == 14:
                    backward_and_norm(i, 0)
                    scores_lo(i, 1)
                if k == 15:
                    ve.wait_ge(hf_rdy, 8 * i + 4)
                    reciprocals(i, 1, 0)
                if k == 16:
                    ve.wait_ge(hn_rdy, 8 * i + 4)
                    backward_and_norm(i, 1)
                if k == 17:
                    ve.wait_ge(unit_out, 20 * i + 4 * (U_B + 4))
                    gated_head(i, 0)
                if k == 18:
                    gated_head(i, 1)
            order.end(PAIRS)
        for c in range(NCH):
            ve.wait_ge(hgs_hi, c + 1)
            less(hglo[:, 4 * c:4 * c + 4, :], hraw[:, c, :, :], hghi[:, 4 * c:4 * c + 4, :]).then_inc(hgs_lo, 1)
        with ve.Fori(0, NCH) as i:
            order.loop(i, 0)
            for k in range(4):
                split(G_C, i, 4, k + 1)
                if k == 3:
                    for n in range(4):
                        ve.wait_ge(cz_in[n % 2], 64 * i + 32 * (n // 2) + 32)
                        ve.wait_ge(sub_done, 16 * i + (4 * (G_C + k) + n + 1))
                        V.tensor_tensor(cz[:, n % 2, 0, :], U[n], cz[:, n % 2, 0, :], ALU.mult)\
                            .then_inc(unit_out, 1)
                        ve.wait_ge(unit_out, 4 * i + (4 * U_C + n + 1))
                        V.tensor_tensor(cz[:, n % 2, 1, :], cz[:, n % 2, 0, :], cz[:, n % 2, 1, :], ALU.add)\
                            .then_inc(z_rdy, 1)
                        ve.wait_ge(z_hi, 4 * i + n + 1)
                        row = bass.ds(4 * i + n, 1)
                        less(zlo[:, row, :], cz[:, n % 2, 1:2, :], zhi[:, row, :]).then_inc(z_lo, 1)
            order.end(NCH)

        def residual(i):
            ve.wait_ge(xc_in, 16 * i + 16)
            for t in range(TT):
                ve.wait_ge(sub_done, 16 * i + (4 * (G_D + 3) + t + 1))
                o = acc[:, t, bass.ds(i * CW, CW)]
                V.scalar_tensor_tensor(o, xc[:, t, :], ALPHA, U[t], ALU.mult, ALU.add).then_inc(unit_out, 1)
            for t in range(TT):
                ve.wait_ge(unit_out, 4 * i + (4 * U_D + t + 1))
                order.add(V.bn_stats(stat[:, t, bass.ds(i, 1), :].rearrange("p a b -> p (a b)"),
                                     acc[:, t, bass.ds(i * CW, CW)]))

        with ve.Fori(0, NCH - 1) as i:
            order.loop(i, TT)
            for k in range(4):
                split(G_D, i, 4, k + 1)
            residual(i)
            order.end(NCH - 1)
        for k in range(3):
            split(G_D + 4 * (NCH - 1), 0, 0, k + 1)
        residual(NCH - 1)

        def norm(var_sem, sq_sem, par_sem, g, b, done):
            order.wait()
            for t in range(TT):
                last_ = V.bn_aggr(mv[:, t, :], stat[:, t, :, :].rearrange("p a b -> p (a b)"))
                if t < TT - 1:
                    order.add(last_)
            last_.then_inc(var_sem, 1)
            order.wait()
            ve.wait_ge(var_sem, 1)
            ve.wait_ge(par_sem, 32)
            for t in range(TT):
                o = acc[:, t, :]
                order.add(V.scalar_tensor_tensor(o, o, mv[:, t, 0:1], g[:, :], ALU.subtract, ALU.mult))
                if t == 0:
                    ve.wait_ge(sq_sem, 1)
                    order.add(V.reciprocal(rstd[:, :], rstd[:, :]))
                order.wait()
                V.scalar_tensor_tensor(o, o, rstd[:, t:t + 1], b[:, :], ALU.mult, ALU.add).then_inc(done, 1)

        norm(var1_rdy, sq1_rdy, ln_in, lng1, lnb1, x1_rdy)
        ve.wait_ge(lg_ps, TT + 1)
        lg = X[1][:, 0:TT * NE].rearrange("p (t e) -> p t e", t=TT)
        order.add(V.reduce_max(sm_max[:, :, 0], lg, AX.X))
        order.wait()
        V.tensor_tensor(sm_exp[:, :, :], lg, sm_max[:, :, :].to_broadcast((P, TT, NE)), ALU.subtract)\
            .then_inc(lg_max, 1)
        ve.wait_ge(lg_exp, 1)
        order.add(V.reduce_sum(sm_sum[:, :, 0], sm_exp[:, :, :], AX.X))
        order.wait()
        order.add(V.reciprocal(sm_sum[:, :, 0], sm_sum[:, :, 0]))
        order.wait()
        V.tensor_tensor(aff_c[:, :, :], sm_exp[:, :, :], sm_sum[:, :, :].to_broadcast((P, TT, NE)), ALU.mult)\
            .then_inc(aff_rdy, 1)
        order.add(V.memset(r_ones[0:NE, :], 1.0))
        ve.wait_ge(affT_ps, 1)
        order.add(V.tensor_copy(aff_r[0:NE, :], X[2][0:NE, :]))
        now = aff_r
        for r in range(CAP // 8):
            order.wait()
            order.add(V.max(top8[0:NE, :], now[0:NE, :]))
            order.wait()
            order.add(V.match_replace(work[r % 2][0:NE, :], top8[0:NE, :], now[0:NE, :], -1.0))
            now = work[r % 2]
        order.wait()
        order.add(V.tensor_tensor(picked[0:NE, :], aff_r[0:NE, :], now[0:NE, :], ALU.not_equal))
        order.wait()
        order.add(V.tensor_tensor_scan(slot_r[0:NE, :], r_ones[0:NE, :], picked[0:NE, :], 0.0, ALU.mult, ALU.add))
        order.wait()
        order.add(V.tensor_tensor(slot_r[0:NE, :], slot_r[0:NE, :], picked[0:NE, :], ALU.mult))
        order.wait()
        V.tensor_scalar(slot_r[0:NE, :], slot_r[0:NE, :], -1.0, None, ALU.add).then_inc(slot_rdy, 1)
        ve.wait_ge(slotT_ps, 1)
        order.add(V.tensor_copy(slot_c[:, :, :].rearrange("p t e -> p (t e)"), X[0][:, 0:TT * NE]))
        order.wait()

        def one_hots(q):
            for e in range(2):
                for t in range(TT):
                    V.tensor_scalar(onehot[:, e, t, :], slot_no[:, :], slot_c[:, t, bass.ds(2 * q + e, 1)], None,
                                    ALU.is_equal).then_inc(oh_rdy, 1)

        def token_numbers(q):
            ve.wait_ge(tok_ps, q + 1)
            V.tensor_copy(tok_f[:, :], X[2][:, 0:1]).then_inc(tok_cp, 1)
            ve.wait_ge(tok_cp, q + 1)
            V.tensor_copy(tok_u[:, :], tok_f[:, :]).then_inc(tok_rdy, 1)

        def tokens_lo(q):
            for b in range(4):
                ve.wait_ge(xeT_hi, 4 * q + b + 1)
                less(xeT[:, 4 * b:4 * b + 4, :, CAP:P], X[b].rearrange("p (r e n) -> p r e n", r=4, e=2),
                     xeT[:, 4 * b:4 * b + 4, :, 0:CAP]).then_inc(xeT_lo, 1)

        def hidden(q, e):
            ve.wait_ge(sig_rdy, 2 * q + e + 1)
            V.tensor_tensor(hid_tmp[:, :], X[0], hid_tmp[:, :], ALU.mult).then_inc(silu_rdy, 1)
            ve.wait_ge(silu_rdy, 2 * q + e + 1)
            ve.wait_ge(guT_ps, 4 * q + 2 * e + 2)
            V.tensor_tensor(hid_tmp[:, :], X[1], hid_tmp[:, :], ALU.mult).then_inc(hid_pre, 1)
            ve.wait_ge(hid_hi, 2 * q + e + 1)
            less(hid[e][:, :, CAP:P], hid_tmp[:, :].rearrange("p (f n) -> p f n", f=FT),
                 hid[e][:, :, 0:CAP]).then_inc(hid_lo, 1)

        def accumulate(q, c):
            ve.wait_ge(comb_ps, 16 * q + 4 * c + 4 + 1)
            o = acc[:, :, c * CW:(c + 1) * CW]
            V.tensor_tensor(o, Xall, o, ALU.add).then_inc(acc_add, 1)

        def statistics(c):
            ve.wait_ge(acc_add, 4 * (EP - 1) + c + 1 + 1)
            for t in range(TT):
                order.add(V.bn_stats(stat[:, t, c, :], acc[:, t, c * CW:(c + 1) * CW]))

        def split_m(q, k):
            ve.wait_ge(hi_done, 48 * q + (G_END + k + 1))
            less(wlo_m[k % HL_M][:, :, :].rearrange("p k n -> p (k n)"), raw_m[k % RAW_M][:, :],
                 whi_m[k % HL_M][:, :, :].rearrange("p k n -> p (k n)")).then_inc(lo_done, 1)

        def steps(q, first, end, last_pair=False):
            for k in range(first, end):
                if k + AHEAD_M < 48:
                    split_m(q, k + AHEAD_M)
                elif not last_pair:
                    split_m(q + 1, k + AHEAD_M - 48)
                if k == 2:
                    ve.wait_ge(gw_ps, q + 1)
                    V.tensor_copy(gate_w[:, :], X[3][:, 0:2]).then_inc(gw_rdy, 1)
                if k == 17:
                    hidden(q, 0)
                if k == 18 and not last_pair:
                    one_hots(q + 1)
                if k == 20 and not last_pair:
                    token_numbers(q + 1)
                if k == 33:
                    hidden(q, 1)
                if k >= 32 and k % 2 == 1:
                    c, e = (k - 32) // 4, (k - 32) % 4 // 2
                    ve.wait_ge(y_hi, 8 * q + 2 * c + e + 1)
                    V.scalar_tensor_tensor(ylo[c % 2][:, e, :], U[2 * e + c % 2], gate_w[:, e:e + 1],
                                           yhi[c % 2][:, e, :].bitcast(F32), ALU.mult, ALU.subtract).then_inc(y_lo, 1)
                if k in (38, 42, 46):
                    accumulate(q, (k - 38) // 4)
                    if last_pair:
                        statistics((k - 38) // 4)
                if k == 34 and not last_pair:
                    tokens_lo(q + 1)

        one_hots(0)
        token_numbers(0)
        for k in range(AHEAD_M):
            split_m(0, k)
        tokens_lo(0)
        ve.wait_ge(acc_scaled, TT)
        steps(0, 0, 2)
        with ve.Fori(0, EP - 1) as i:
            steps(i, 2, 48)
            steps(i + 1, 0, 2)
            accumulate(i, 3)
        steps(EP - 1, 2, 48, True)
        accumulate(EP - 1, 3)
        statistics(3)
        norm(o_var, o_sq, ln2_in, lng2, lnb2, o_rdy)

    keep.close()


_INS = ["x", "w_in", "b_if", "w_pool_grp", "pool_scale", "w_pool_up", "mlstm_norm_w", "w_mlstm_up", "w_out",
        "ln1_g", "ln1_b", "w_router", "w_gate", "w_up", "w_down", "ln2_g", "ln2_b"]


def kernel(**inputs):
    import concourse.bacc as bacc
    import numpy as np
    from concourse.bass_utils import run_bass_kernel_spmd

    nc = bacc.Bacc("TRN2", target_bir_lowering=False, num_devices=1)
    arrays, args = {}, []
    for name in _INS:
        a = np.ascontiguousarray(inputs[name])
        arrays[f"in_{name}"] = a
        args.append(nc.dram_tensor(f"in_{name}", a.shape, mybir.dt.from_np(a.dtype), kind="ExternalInput").ap())
    args.append(nc.dram_tensor("out_x", (1, S, D), F32, kind="ExternalOutput").ap())
    build(nc, args)
    r = run_bass_kernel_spmd(nc, [arrays], core_ids=[0])
    return r.results[0]["out_x"]
```
